# Optimizing a Trainium2 kernel written in Bass

```python
import math
import jax, jax.numpy as jnp
from jax import lax
import numpy as np

D_MODEL = 1024
BATCH = 1
SEQ = 256
DEPTH = 1

CHUNK = 64
SWA_HEADS = 16
SWA_KV_HEADS = 4
SWA_HEAD_DIM = 64
SWA_WINDOW = 128
SWA_WIN_CHUNKS = SWA_WINDOW // CHUNK
GDN_HEADS = 8
GDN_DK = 128
GDN_DV = 128
CONV_K = 4
N_GROUPS = 4
EXPERTS_PER_GROUP = 8
N_EXPERTS = N_GROUPS * EXPERTS_PER_GROUP
TOP_K = 2
D_EXPERT = 256
PLE_DIM = 256

LN_EPS = 1e-5
NORM_EPS = 1e-6
NEG_INF = -1e30
DN_ALPHA = (2 * DEPTH) ** 0.25
DN_BETA = (8 * DEPTH) ** -0.25

A_Q = SWA_HEADS * SWA_HEAD_DIM
A_KV = SWA_KV_HEADS * SWA_HEAD_DIM
B_QK = GDN_HEADS * GDN_DK
B_V = GDN_HEADS * GDN_DV
B_QKV = 2 * B_QK + B_V
SPLIT_SIZES = (A_Q, A_KV, A_KV, B_QKV, B_V, GDN_HEADS, GDN_HEADS, D_MODEL, D_MODEL)
IN_WIDTH = sum(SPLIT_SIZES)

kernel_name = 'hybrid_swa_sink_gdn_hmoe_deepnorm_block'

def layer_norm(x, g, b):
    xf = x.astype(jnp.float32)
    mu = jnp.mean(xf, axis=-1, keepdims=True)
    xc = xf - mu
    var = jnp.mean(xc * xc, axis=-1, keepdims=True)
    y = xc * lax.rsqrt(var + LN_EPS) * g.astype(jnp.float32) + b.astype(jnp.float32)
    return y.astype(x.dtype)

def l2norm(x):
    return x * lax.rsqrt(jnp.sum(x * x, axis=-1, keepdims=True) + NORM_EPS)

def swa_sink_attention(q, k, v, sink):
    B, T = q.shape[0], q.shape[1]
    n_c = T // CHUNK
    G = SWA_HEADS // SWA_KV_HEADS
    W = SWA_WIN_CHUNKS
    qc = q.reshape(B, n_c, CHUNK, SWA_KV_HEADS, G, SWA_HEAD_DIM)
    kc = k.reshape(B, n_c, CHUNK, SWA_KV_HEADS, SWA_HEAD_DIM)
    vc = v.reshape(B, n_c, CHUNK, SWA_KV_HEADS, SWA_HEAD_DIM)
    pad = ((0, 0), (W - 1, 0), (0, 0), (0, 0), (0, 0))
    kp = jnp.pad(kc, pad)
    vp = jnp.pad(vc, pad)
    kb = jnp.concatenate([kp[:, w:w + n_c] for w in range(W)], axis=2)
    vb = jnp.concatenate([vp[:, w:w + n_c] for w in range(W)], axis=2)
    slot_chunk = jnp.arange(W * CHUNK)[None, :] // CHUNK
    valid = (jnp.arange(n_c)[:, None] + slot_chunk - (W - 1)) >= 0
    s = jnp.einsum('bcqhgd,bckhd->bchgqk', qc, kb, preferred_element_type=jnp.float32)
    s = s * (SWA_HEAD_DIM ** -0.5)
    s = jnp.where(valid[None, :, None, None, None, :], s, NEG_INF)
    sk = sink.astype(jnp.float32).reshape(SWA_KV_HEADS, G)[None, None, :, :, None, None]
    m = jnp.maximum(jnp.max(s, axis=-1, keepdims=True), sk)
    pr = jnp.exp(s - m)
    den = jnp.sum(pr, axis=-1, keepdims=True) + jnp.exp(sk - m)
    pr = (pr / den).astype(v.dtype)
    o = jnp.einsum('bchgqk,bckhd->bcqhgd', pr, vb)
    return o.reshape(B, T, SWA_HEADS * SWA_HEAD_DIM)

def causal_short_conv(x, w):
    C = x.shape[-1]
    y = lax.conv_general_dilated(x, w[:, None, :].astype(x.dtype), window_strides=(1,),
                                 padding=[(CONV_K - 1, 0)],
                                 dimension_numbers=('NWC', 'WIO', 'NWC'),
                                 feature_group_count=C)
    return jax.nn.silu(y)

def gated_delta_rule(q, k, v, g, beta):
    B, T, H, dk = q.shape
    dv = v.shape[-1]
    n_c = T // CHUNK

    def chunks(a):
        return a.reshape(B, n_c, CHUNK, H, -1).transpose(0, 3, 1, 2, 4)

    q = chunks(q) * (dk ** -0.5)
    k = chunks(k)
    v = chunks(v)
    g = g.reshape(B, n_c, CHUNK, H).transpose(0, 3, 1, 2)
    beta = beta.reshape(B, n_c, CHUNK, H).transpose(0, 3, 1, 2)
    gc = jnp.cumsum(g, axis=-1)
    tril = jnp.tril(jnp.ones((CHUNK, CHUNK), dtype=bool))
    strict = jnp.tril(jnp.ones((CHUNK, CHUNK), dtype=bool), -1)
    diff = gc[..., :, None] - gc[..., None, :]
    decay = jnp.where(tril, jnp.exp(jnp.where(tril, diff, 0.0)), 0.0)
    k_beta = k * beta[..., None]
    L = jnp.where(strict, jnp.einsum('bhnid,bhnjd->bhnij', k_beta, k) * decay, 0.0)
    eye = jnp.eye(CHUNK, dtype=jnp.float32)
    t_inv = lax.linalg.triangular_solve(eye + L, jnp.broadcast_to(eye, L.shape),
                                        left_side=True, lower=True, unit_diagonal=True)
    u = jnp.einsum('bhnij,bhnjd->bhnid', t_inv, v * beta[..., None])
    w = jnp.einsum('bhnij,bhnjd->bhnid', t_inv, k_beta * jnp.exp(gc)[..., None])
    a_intra = jnp.where(tril, jnp.einsum('bhnid,bhnjd->bhnij', q, k) * decay, 0.0)
    q_dec = q * jnp.exp(gc)[..., None]
    k_dec = k * jnp.exp(gc[..., -1:] - gc)[..., None]
    g_last = jnp.exp(gc[..., -1])

    def step(S, inp):
        w_c, u_c, qd_c, kd_c, a_c, gl_c = inp
        v_new = u_c - w_c @ S
        o_c = qd_c @ S + a_c @ v_new
        S = S * gl_c[..., None, None] + jnp.swapaxes(kd_c, -1, -2) @ v_new
        return S, o_c

    mv = lambda a: jnp.moveaxis(a, 2, 0)
    xs = (mv(w), mv(u), mv(q_dec), mv(k_dec), mv(a_intra), jnp.moveaxis(g_last, 2, 0))
    S0 = jnp.zeros((B, H, dk, dv), jnp.float32)
    _, o = lax.scan(step, S0, xs)
    return o.transpose(1, 0, 3, 2, 4).reshape(B, T, H, dv)

def gated_deltanet(qkv, z, beta_logit, a_logit, conv_w, a_log, dt_bias, norm_g):
    B, T = qkv.shape[0], qkv.shape[1]
    out_dtype = qkv.dtype
    h = causal_short_conv(qkv, conv_w).astype(jnp.float32)
    q = l2norm(h[..., :B_QK].reshape(B, T, GDN_HEADS, GDN_DK))
    k = l2norm(h[..., B_QK:2 * B_QK].reshape(B, T, GDN_HEADS, GDN_DK))
    v = h[..., 2 * B_QK:].reshape(B, T, GDN_HEADS, GDN_DV)
    g = -jnp.exp(a_log.astype(jnp.float32)) * jax.nn.softplus(
        a_logit.astype(jnp.float32) + dt_bias.astype(jnp.float32))
    beta = jax.nn.sigmoid(beta_logit.astype(jnp.float32))
    o = gated_delta_rule(q, k, v, g, beta)
    o = o * lax.rsqrt(jnp.mean(o * o, axis=-1, keepdims=True) + NORM_EPS) * norm_g.astype(jnp.float32)
    o = o * jax.nn.silu(z.astype(jnp.float32)).reshape(B, T, GDN_HEADS, GDN_DV)
    return o.reshape(B, T, B_V).astype(out_dtype)

def hierarchical_moe(h, w_rg, b_rg, w_re, b_re, w_gate, w_up, w_down):
    B, T, D = h.shape
    hf = h.reshape(-1, D)
    n_tok = hf.shape[0]
    g_logit = (hf @ w_rg + b_rg).astype(jnp.float32)
    g_prob = jax.nn.softmax(g_logit, axis=-1)
    g_val, g_idx = lax.top_k(g_prob, 1)
    e_logit = (hf @ w_re + b_re).astype(jnp.float32).reshape(n_tok, N_GROUPS, EXPERTS_PER_GROUP)
    e_logit = jnp.take_along_axis(e_logit, g_idx[:, :, None], axis=1)[:, 0]
    e_prob = jax.nn.softmax(e_logit, axis=-1)
    top_w, top_i = lax.top_k(e_prob, TOP_K)
    top_w = top_w / jnp.sum(top_w, axis=-1, keepdims=True)
    expert_id = g_idx * EXPERTS_PER_GROUP + top_i
    weights = g_val * top_w
    combine = jnp.sum(jax.nn.one_hot(expert_id, N_EXPERTS, dtype=jnp.float32) * weights[..., None], axis=1)
    combine = combine.astype(hf.dtype)
    out = jnp.zeros_like(hf)
    for e in range(N_EXPERTS):
        he = jax.nn.silu(hf @ w_gate[e]) * (hf @ w_up[e])
        out = out + combine[:, e:e + 1] * (he @ w_down[e])
    return out.reshape(B, T, D)

def setup_inputs(seed: int = 0) -> dict:
    key = jax.random.key(seed)
    ks = jax.random.split(key, 32)
    L = DEPTH
    f32 = jnp.float32

    def nrm(k, shape, fan_in, scale=1.0):
        return jax.random.normal(k, shape, f32) * (scale * fan_in ** -0.5)

    def gain(k, shape):
        return 1.0 + 0.02 * jax.random.normal(k, shape, f32)

    def bias(k, shape):
        return 0.01 * jax.random.normal(k, shape, f32)

    x = jax.random.normal(ks[0], (BATCH, SEQ, D_MODEL), f32)
    p = jax.random.normal(ks[1], (DEPTH, BATCH, SEQ, PLE_DIM), f32)
    w_in = nrm(ks[2], (L, D_MODEL, IN_WIDTH), D_MODEL)
    attn_sink = 0.5 * jax.random.normal(ks[3], (L, SWA_HEADS), f32)
    conv_w = nrm(ks[4], (L, CONV_K, B_QKV), CONV_K)
    a_log = jnp.log(jax.random.uniform(ks[5], (L, GDN_HEADS), f32, minval=1.0, maxval=16.0))
    dt = jnp.exp(jax.random.uniform(ks[6], (L, GDN_HEADS), f32)
                 * (math.log(0.1) - math.log(0.001)) + math.log(0.001))
    dt_bias = dt + jnp.log(-jnp.expm1(-dt))
    gdn_norm_g = gain(ks[7], (L, GDN_DV))
    w_branch_a = nrm(ks[8], (L, A_Q, D_MODEL), A_Q, DN_BETA)
    w_branch_b = nrm(ks[9], (L, B_V, D_MODEL), B_V, DN_BETA)
    w_out = nrm(ks[10], (L, D_MODEL, D_MODEL), D_MODEL, DN_BETA)
    ln1_g = gain(ks[11], (L, D_MODEL))
    ln1_b = bias(ks[12], (L, D_MODEL))
    w_route_group = nrm(ks[13], (L, D_MODEL, N_GROUPS), D_MODEL)
    b_route_group = bias(ks[14], (L, N_GROUPS))
    w_route_expert = nrm(ks[15], (L, D_MODEL, N_EXPERTS), D_MODEL)
    b_route_expert = bias(ks[16], (L, N_EXPERTS))
    w_exp_gate = nrm(ks[17], (L, N_EXPERTS, D_MODEL, D_EXPERT), D_MODEL)
    w_exp_up = nrm(ks[18], (L, N_EXPERTS, D_MODEL, D_EXPERT), D_MODEL)
    w_exp_down = nrm(ks[19], (L, N_EXPERTS, D_EXPERT, D_MODEL), D_EXPERT, DN_BETA)
    w_ple_gate = nrm(ks[20], (L, D_MODEL, D_MODEL), D_MODEL)
    b_ple_gate = bias(ks[21], (L, D_MODEL))
    w_ple_proj = nrm(ks[22], (L, PLE_DIM, D_MODEL), PLE_DIM, DN_BETA)
    ln2_g = gain(ks[23], (L, D_MODEL))
    ln2_b = bias(ks[24], (L, D_MODEL))
    return {'x': x, 'p': p, 'w_in': w_in, 'attn_sink': attn_sink, 'conv_w': conv_w,
            'a_log': a_log, 'dt_bias': dt_bias, 'gdn_norm_g': gdn_norm_g,
            'w_branch_a': w_branch_a, 'w_branch_b': w_branch_b, 'w_out': w_out,
            'ln1_g': ln1_g, 'ln1_b': ln1_b,
            'w_route_group': w_route_group, 'b_route_group': b_route_group,
            'w_route_expert': w_route_expert, 'b_route_expert': b_route_expert,
            'w_exp_gate': w_exp_gate, 'w_exp_up': w_exp_up, 'w_exp_down': w_exp_down,
            'w_ple_gate': w_ple_gate, 'b_ple_gate': b_ple_gate, 'w_ple_proj': w_ple_proj,
            'ln2_g': ln2_g, 'ln2_b': ln2_b}

def reference(x, p, w_in, attn_sink, conv_w, a_log, dt_bias, gdn_norm_g,
              w_branch_a, w_branch_b, w_out, ln1_g, ln1_b,
              w_route_group, b_route_group, w_route_expert, b_route_expert,
              w_exp_gate, w_exp_up, w_exp_down,
              w_ple_gate, b_ple_gate, w_ple_proj, ln2_g, ln2_b):
    B, T, _ = x.shape
    split_points = np.cumsum(SPLIT_SIZES)[:-1].tolist()
    h = x
    for i in range(DEPTH):
        proj = h @ w_in[i]
        qa, ka, va, qkv_b, z_b, beta_logit, a_logit, gate_a, gate_b = jnp.split(proj, split_points, axis=-1)
        ya = swa_sink_attention(qa.reshape(B, T, SWA_HEADS, SWA_HEAD_DIM),
                                ka.reshape(B, T, SWA_KV_HEADS, SWA_HEAD_DIM),
                                va.reshape(B, T, SWA_KV_HEADS, SWA_HEAD_DIM),
                                attn_sink[i])
        yb = gated_deltanet(qkv_b, z_b, beta_logit, a_logit, conv_w[i], a_log[i], dt_bias[i], gdn_norm_g[i])
        merged = jax.nn.sigmoid(gate_a) * (ya @ w_branch_a[i]) + jax.nn.sigmoid(gate_b) * (yb @ w_branch_b[i])
        h = layer_norm(DN_ALPHA * h + merged @ w_out[i], ln1_g[i], ln1_b[i])
        ffn = hierarchical_moe(h, w_route_group[i], b_route_group[i], w_route_expert[i], b_route_expert[i],
                               w_exp_gate[i], w_exp_up[i], w_exp_down[i])
        ple = jax.nn.sigmoid(h @ w_ple_gate[i] + b_ple_gate[i]) * (p[i] @ w_ple_proj[i])
        h = layer_norm(DN_ALPHA * h + ffn + ple, ln2_g[i], ln2_b[i])
    return h


_drawn_inputs = setup_inputs


def setup_inputs(seed=0):
    import zlib

    import numpy as np

    out = dict(_drawn_inputs(seed))
    spreads = {}
    factors = {'attn_sink': 60.761,
     'gdn_norm_g': 32.944,
     'ln1_b': 4.647,
     'b_route_group': 22.204,
     'b_route_expert': 7.131,
     'b_ple_gate': 200.0,
     'ln2_g': 24.537,
     'ln2_b': 48.139,
     'w_branch_a': 2.79,
     'ln1_g': 2.67}
    for name, (base, spread) in spreads.items():
        noise = np.random.default_rng([zlib.crc32(name.encode()), seed]).standard_normal(out[name].shape)
        drawn = base * np.exp(spread * noise) if base else spread * noise
        out[name] = __import__('jax').numpy.asarray(drawn.astype(out[name].dtype))
    for name, factor in factors.items():
        out[name] = (out[name] * factor).astype(out[name].dtype)
    return out
```

```python
import math
from contextlib import ExitStack

import concourse.bass as bass
from concourse import mybir
from concourse.alu_op_type import AluOpType as ALU

F32 = mybir.dt.float32
F32R = mybir.dt.float32r
I32 = mybir.dt.int32
U32 = mybir.dt.uint32
ACT = mybir.ActivationFunctionType
AX_X = mybir.AxisListType.X

P = 128
KB = 1024
D = 1024
T = 256
TT = T // P
KT = D // P
C = 64
NC = T // C
ATT_SLICES = ((3, 2, 1), (5, 2, 2), (5, 2, 2), (5, 2, 1))
H = 8
HP = 8
KVH = 4
TAPS = 4
U = H * TT
N_EXP = 32
N_GRP = 4
EPG = N_EXP // N_GRP
F = 256
SLOTS = 64
PASSES = T // SLOTS
PLE = 256
ALPHA = 2.0 ** 0.25
LN_EPS = 1e-5
NORM_EPS = 1e-6
BIG = 1e30
W = 512

QA, KA, VA, QB, KB_, VB, ZB, BETA, GA, GB = 0, 1024, 1280, 1536, 2560, 3584, 4608, 5632, 5648, 6672

LEAD = 5
RING = 8
CHUNK = 4
RAWS = 4


def plan_blocks():
    b = [("ab", "x", KT, BETA, 16)]
    b += [("k", "x", KT, KB_ + W * i, W) for i in range(2)]
    b += [("q", "x", KT, QB + W * i, W) for i in range(2)]
    b += [("v", "x", KT, VB + W * i, W) for i in range(2)]
    b += [("qa", "x", KT, QA + W * i, W) for i in range(2)]
    b += [("kva", "x", KT, KA, W)]
    b += [("z", "x", KT, ZB + W * i, W) for i in range(2)]
    b += [("ga", "x", KT, GA + W * i, W) for i in range(2)]
    b += [("gb", "x", KT, GB + W * i, W) for i in range(2)]
    b += [("wb", "yb", KT, W * i, W) for i in range(2)]
    b += [("wa", "ya", KT, W * i, W) for i in range(2)]
    b += [("wo", "m", KT, W * i, W) for i in range(2)]
    b += [("rt", "h", KT, 0, N_GRP + N_EXP)]
    b += [("pg", "h", KT, W * i, W) for i in range(2)]
    b += [("pp", "p", 2, W * i, W) for i in range(2)]
    return b


def build(nc, x, p, w_in, attn_sink, conv_w, a_log, dt_bias, gdn_norm_g, w_branch_a, w_branch_b, w_out,
          ln1_g, ln1_b, w_route_group, b_route_group, w_route_expert, b_route_expert,
          w_exp_gate, w_exp_up, w_exp_down, w_ple_gate, b_ple_gate, w_ple_proj, ln2_g, ln2_b, out):
    blocks = plan_blocks()
    names = [b[0] for b in blocks]
    slices = [(b, kt) for b, blk in enumerate(blocks) for kt in range(blk[2])]
    first_slice = [next(j for j, s in enumerate(slices) if s[0] == b) for b in range(len(blocks))]
    loads, place = [], {}
    for b, blk in enumerate(blocks):
        for k0 in range(0, blk[2], CHUNK):
            n = min(CHUNK, blk[2] - k0)
            for k in range(n):
                place[first_slice[b] + k0 + k] = (len(loads), k)
            loads.append((b, k0, n))
    last_slice_of = [max(j for j in place if place[j][0] == m) for m in range(len(loads))]

    ctx = ExitStack()
    with ctx:
        BASE = 17 * KB
        cursor = [BASE]

        def at(name, shape, dt, off):
            return nc.alloc_sbuf_tensor_at(name, shape, dt, offset=off)

        def perm(name, shape, dt=F32):
            n = 4
            for s in shape[1:]:
                n *= s
            off = cursor[0]
            cursor[0] += (n + 31) // 32 * 32
            return at(name, shape, dt, off)

        ident = perm("ident", [P, P])
        tri = perm("tri", [P, P])
        before = perm("before", [P, P])
        chunk1 = perm("chunk1", [P, P])
        half_rows = perm("half_rows", [P, 2, P])
        ones = perm("ones", [P, P])
        stack_eye = perm("stack_eye", [P, C])
        level_mask = perm("level_mask", [P, 6, C])
        mask_upper = perm("mask_upper", [P, C])
        mask_sub = perm("mask_sub", [P, C])
        conv_rows = perm("conv_rows", [P, P])
        conv_c = perm("conv_c", [P, TAPS, 24])
        sink = perm("sink", [P, HP])
        sink_all = perm("sink_all", [P, 2 * HP])
        alog = perm("alog", [P, H])
        dtb = perm("dtb", [P, H])
        norm_g = perm("norm_g", [P, P])
        ab = perm("ab", [P, TT, 16])
        beta = perm("beta", [P, TT, H])
        beta_half = perm("beta_half", [P, TT, H])
        soft = perm("soft", [P, TT, H])
        softb = perm("softb", [P, TT, H])
        decay_g = perm("decay_g", [P, TT, H])
        neg_a = perm("neg_a", [P, H])
        gc = perm("gc", [P, TT, H])
        to_end = perm("to_end", [P, TT, H])
        g_chunk = perm("g_chunk", [P, NC, H])
        smax = perm("smax", [P, 2, HP])
        sden = perm("sden", [P, 2, HP])
        sexp = perm("sexp", [P, 2, HP])
        o_sum = perm("o_sum", [P, TT, H])
        o_rs = perm("o_rs", [P, TT, H])
        stats = perm("stats", [P, TT, 2, 6])
        mv = perm("mv", [P, TT, 2])
        rstd = perm("rstd", [P, TT])
        eps_l2 = perm("eps_l2", [P, 1])
        eps_ln = perm("eps_ln", [P, 1])
        eps_norm = perm("eps_norm", [P, 1])
        one = perm("one", [P, 1])
        rt_b = perm("rt_b", [P, N_GRP + N_EXP])
        iota_e = perm("iota_e", [P, N_EXP])
        iota_s = perm("iota_s", [P, SLOTS])
        lg = perm("lg", [P, TT, N_GRP + N_EXP])
        g8 = perm("g8", [P, TT, 8])
        top8 = perm("top8", [P, TT, 2, 8])
        idx8 = perm("idx8", [P, TT, 2, 8], U32)
        idxf = perm("idxf", [P, TT, 2, 8])
        g_hot = perm("g_hot", [P, TT, N_GRP])
        e_mask = perm("e_mask", [P, TT, N_GRP, EPG])
        hot = perm("hot", [P, 2, TT, N_EXP])
        r_small = perm("r_small", [P, 8, TT])
        picked = perm("picked", [P, TT, N_EXP])
        comb = perm("comb", [P, TT, N_EXP + 2])
        posm = perm("posm", [P, TT, N_EXP + 2])
        n_tok = perm("n_tok", [P, N_EXP])
        n_max = perm("n_max", [P, 1])
        more = perm("more", [P, 1], I32)
        w_slot = perm("w_slot", [P, 2])
        STREAM = (cursor[0] + 127) // 128 * 128
        raw = at("raw", [P, RAWS, CHUNK, W], F32, STREAM)
        w_hi = at("w_hi", [P, RING, W], F32R, STREAM + 32 * KB)
        w_lo = at("w_lo", [P, RING, W], F32R, STREAM + 48 * KB)
        XT = STREAM + 64 * KB
        A0 = XT + 16 * KB

        def area(name, shape, kb, dt=F32):
            return at(name, shape, dt, A0 + int(kb * KB))

        def pair(name, off, kt=KT):
            return (at(name + "_hi", [P, kt, T], F32R, off), at(name + "_lo", [P, kt, T], F32R, off + kt * KB))

        pairs = {"x": pair("xT", XT), "ya": pair("yaT", A0 + 76 * KB), "yb": pair("ybT", A0),
                 "m": pair("mT", XT), "h": pair("hT", A0 + 76 * KB), "p": pair("pT", A0 + 110 * KB, 2)}
        x_tok = area("x_tok", [P, TT, D], 92)
        kbT = area("kbT", [P, H, T], 0)
        qT = area("qT", [P, H, T], 8)
        vb = area("vb", [P, TT, D], 16)
        kdec = area("kdec", [P, TT, D], 24)
        invT = area("invT", [P, U, C], 32)
        attT = area("attT", [P, U, C], 36)
        S = area("S", [P, H, P], 40)
        R = area("R", [P, D], 44)
        v_new = area("v_new", [P, D], 48)
        o_tok = area("o_tok", [P, TT, D], 52)
        zg = area("zg", [P, TT, D], 60)
        th_a = area("th_a", [P, TT, D], 68)
        conv_in = area("conv_in", [P, 2, 4, TAPS - 1 + T], 60)
        conv_y = area("conv_y", [P, 4, T], 44)
        conv_t = area("conv_t", [P, 4, T], 48)
        sq = area("sq", [P, 4, T], 40)
        rs = area("rs", [P, 2, 4, T], 52)
        kT = area("kT", [P, H, T], 76)
        vT = area("vT", [P, H, T], 84)
        eg = area("eg", [P, H, T], 68)
        dec_sub = area("dec_sub", [P, U, C], 52)
        dec_up = area("dec_up", [P, U, C], 56)
        LT = area("LT", [P, U, C], 40)
        prod = area("prod", [P, U, C], 44)
        inv = area("inv", [P, U, C], 48)
        LT_lev = area("LT_lev", [P, 2, U, C], 52)
        qaT = area("qaT", [P, HP, T], 92)
        kaT = area("kaT", [P, KVH, T], 100)
        va = area("va", [P, 3, 256], 104)
        pr = area("pr", [P, HP, P], 107)
        prT = area("prT", [P, HP, P], 111)
        th_b = area("th_b", [P, TT, D], 40)
        merged = area("merged", [P, TT, D], 16)
        gated_a = area("gated_a", [P, TT, W], 92)
        x_again = area("x_again", [P, TT, D], 24)
        h_tok = area("h_tok", [P, TT, D], 32)
        ln1g = area("ln1g", [P, D], 100)
        ln1b = area("ln1b", [P, D], 104)
        p_tok = area("p_tok", [P, TT, PLE], 108)
        pleb = area("pleb", [P, D], 72)
        ln2g = area("ln2g", [P, D], 24)
        ln2b = area("ln2b", [P, D], 28)
        gu_off = [A0, A0 + 40 * KB, A0 + 56 * KB, STREAM]
        dn_off = [A0 + 16 * KB, A0 + 92 * KB, A0 + 100 * KB, STREAM + 16 * KB]
        w_gu = [at(f"w_gu{s}", [P, KT, 2, F], F32, gu_off[s]) for s in range(4)]
        w_dn = [at(f"w_dn{s}", [P, 2, D], F32, dn_off[s]) for s in range(4)]
        acc = at("acc", [P, TT, D], F32, XT)
        th_p = at("th_p", [P, TT, D], F32, XT + 8 * KB)
        hk_hi = at("hk_hi", [P, TT, D], F32R, STREAM + 32 * KB)
        hk_lo = at("hk_lo", [P, TT, D], F32R, STREAM + 40 * KB)
        M0 = STREAM + 48 * KB
        gath = at("gath", [P, KT, P], F32, M0)
        y_hi = at("y_hi", [P, D], F32R, M0 + 4 * KB)
        y_lo = at("y_lo", [P, D], F32R, M0 + 8 * KB)
        gus = at("gus", [P, 2, W], F32, M0 + 12 * KB)
        M1 = STREAM + 24 * KB
        sg = at("sg", [P, 2, 2, SLOTS], F32, M1)
        he = at("he", [P, 2, 2, SLOTS], F32, M1 + 1 * KB)
        sel = at("sel", [P, TT, P], F32R, M1 + 2 * KB)
        selT = at("selT", [P, 2, TT, P], F32R, M1 + 3 * KB)

        psD = ctx.enter_context(nc.psum_tensor("psD", [P, 4, 512], F32))
        psX = ctx.enter_context(nc.psum_tensor("psX", [P, 4, 512], F32))
        xbank = psX[:].rearrange("p b n -> p (b n)")
        dbank = psD[:].rearrange("p b n -> p (b n)")

        def sem(name):
            return ctx.enter_context(nc.semaphore(name))

        load_sem = [sem(f"raw_loaded{m}") for m in range(RAWS)]
        hi_ready, lo_ready, slice_used = sem("hi_ready"), sem("lo_ready"), sem("slice_used")
        block_done, block_read = sem("block_done"), sem("block_read")
        x_loaded, small_loaded, bias_loaded = sem("x_loaded"), sem("small_loaded"), sem("bias_loaded")
        ident_ready, biases_ready, consts = sem("ident_ready"), sem("biases_ready"), sem("consts")
        tr_done, hi_made, lo_made = sem("transposed"), sem("pair_hi_made"), sem("pair_lo_made")
        vec, act_s, pool_s = sem("vector_chain"), sem("scalar_chain"), sem("pool_chain")

        def wait(eng, s, v):
            if not isinstance(v, int) or v > 0:
                eng.wait_ge(s, v)

        def chain(eng, s):
            n = [0]

            def link(ins):
                n[0] += 1
                ins.then_inc(s, 1)
                return ins

            def settle():
                if n[0]:
                    eng.wait_ge(s, n[0])
            return link, settle

        kv_b = names.index("kva")
        last = {n: len(names) - 1 - names[::-1].index(n) for n in set(names)}
        end_slice = {first_slice[b] + blk[2] - 1: b for b, blk in enumerate(blocks)}
        lo_needed = {"x": 4, "yb": 8, "m": 12, "h": 16}

        conv_ready, conv_th, conv_out = sem("conv_ready"), sem("conv_tanh"), sem("conv_out")
        squared, sq_summed, rs_ready, normed = sem("squared"), sem("sq_summed"), sem("rs_ready"), sem("normed")
        cw_tr, cw_ready = sem("conv_taps_turned"), sem("conv_taps_ready")
        ab1, ab2, ab3, ab4, beta_ready = (sem("soft_in"), sem("soft_exp"), sem("decay_ready"), sem("beta_exp"),
                                          sem("beta_ready"))
        cum_done, cum_read, cum_exp = sem("cum_done"), sem("cum_read"), sem("cum_exp")
        brow, kb_ready = sem("beta_rows"), sem("kb_ready")
        grow, eg_ready, dec_raw, dec_masked, dec_ready = (sem("gc_rows"), sem("eg_ready"), sem("dec_raw"),
                                                          sem("dec_masked"), sem("dec_ready"))
        gram, gram_read, eg_used = sem("grams"), sem("grams_read"), sem("eg_applied")
        vtr, vb_ready, ktr, kdec_ready = sem("v_turned"), sem("vb_ready"), sem("k_turned"), sem("kdec_ready")
        lev_masked, lev_prod, lev_copied, lev_join, inv_ready = (
            sem("level_masked"), sem("level_product"), sem("level_copied"), sem("level_joined"), sem("inverse_level"))
        ks_done, r_ready, vn_done, vn_ready, o_done, o_read, ds_done, s_scaled, s_ready = (
            sem("ks_done"), sem("r_ready"), sem("vn_done"), sem("vn_ready"), sem("o_done"), sem("o_read"),
            sem("ds_done"), sem("s_scaled"), sem("s_ready"))
        o_squared, o_summed, o_rs_ready, o_final = sem("o_squared"), sem("o_summed"), sem("o_rs"), sem("o_final")
        o_gated = sem("o_gated")
        sc_done, sc_shift, sc_exp, sc_den, pr_ready, pt_done, pt_read, pv_done, ya_hi, ya_made = (
            sem("scores_done"), sem("scores_shifted"), sem("scores_exp"), sem("scores_den"), sem("probs_ready"),
            sem("probs_turned"), sem("probs_turned_read"), sem("pv_done"), sem("ya_hi"), sem("ya_made"))
        z_th, z_norm, ax_ready, x2_loaded, ln1_loaded = (sem("z_tanh"), sem("z_norm"), sem("ax_ready"),
                                                         sem("x_again_loaded"), sem("ln1_loaded"))
        gb_ready, merged_ready = sem("gated_a_ready"), sem("merged_ready")
        ln_var, ln_rstd, ln_centred, h_ready = sem("ln_var"), sem("ln_rstd"), sem("ln_centred"), sem("h_ready")
        p_loaded, p_turned, p_hi, p_made = sem("p_loaded"), sem("p_turned"), sem("p_hi"), sem("p_made")
        pleb_loaded, ln2_loaded, pg_in, pg_th = sem("pleb_loaded"), sem("ln2_loaded"), sem("ple_in"), sem("ple_tanh")
        acc_scaled, hk_hi_ready, hk_ready = sem("acc_scaled"), sem("hk_hi_ready"), sem("hk_ready")
        rt_in, rt_exp, rt_picked, rt_cum, rt_done = (sem("route_logits"), sem("route_exp"), sem("route_picked"),
                                                     sem("route_cum"), sem("route_done"))
        gu_load = [sem(f"w_gu_loaded{s_}") for s_ in range(4)]
        dn_load = [sem(f"w_dn_loaded{s_}") for s_ in range(4)]
        sel_ready, gather_done, gath_ready, gu_done, gus_ready, t_done, silu_done, he_ready = (
            sem("sel_ready"), sem("gather_done"), sem("gathered_ready"), sem("gate_up_done"), sem("gate_up_read"),
            sem("turned_done"), sem("silu_done"), sem("hidden_ready"))
        dn_done, yhi_ready, ylo_ready, selt_done, selt_ready, sc_out, acc_added = (
            sem("down_done"), sem("y_hi_ready"), sem("y_lo_ready"), sem("sel_turned"), sem("sel_turned_read"),
            sem("scattered"), sem("acc_added"))
        stored, sink_ready, z_free, pass_shift = sem("stored"), sem("sink_ready"), sem("norm_gain_halved"), sem("pass_shift")
        o_sq = area("o_sq", [P, TT, D], 40)
        load_counts, totals = [], [0] * RAWS
        for m, (b_, _, _) in enumerate(loads):
            totals[m % RAWS] += 32 if names[b_] == "rt" else 16
            load_counts.append(totals[m % RAWS])

        def load_count(m):
            return load_counts[m]

        def dtb_rows():
            return dtb[:].unsqueeze(1).to_broadcast([P, TT, H])

        def neg_rows():
            return neg_a[:].unsqueeze(1).to_broadcast([P, TT, H])

        def win_slices(b, k0, n):
            name, _, _, off, wd = blocks[b]
            src = {"wa": w_branch_a, "wb": w_branch_b, "wo": w_out, "pg": w_ple_gate, "pp": w_ple_proj}.get(name, w_in)
            return src[0].rearrange("(k p) n -> p k n", p=P)[:, k0:k0 + n, off:off + wd]

        def bc(ap, dims):
            return ap.to_broadcast(dims)

        block = ctx.enter_context(nc.Block())

        @block.sync
        def _(sp):
            sp.dma_start(x_tok[:], x[0].rearrange("(t p) d -> p t d", p=P)).then_inc(x_loaded, 16)

            def load(m):
                b, k0, n = loads[m]
                wd = blocks[b][4]
                if m >= RAWS:
                    sp.wait_ge(lo_ready, last_slice_of[m - RAWS] + 1)
                dst = raw[:, m % RAWS, 0:n, 0:wd]
                if names[b] == "rt":
                    rg = w_route_group[0].rearrange("(k p) n -> p k n", p=P)[:, k0:k0 + n]
                    re = w_route_expert[0].rearrange("(k p) n -> p k n", p=P)[:, k0:k0 + n]
                    sp.dma_start(raw[:, m % RAWS, 0:n, 0:N_GRP], rg).then_inc(load_sem[m % RAWS], 16)
                    sp.dma_start(raw[:, m % RAWS, 0:n, N_GRP:N_GRP + N_EXP], re).then_inc(load_sem[m % RAWS], 16)
                else:
                    sp.dma_start(dst, win_slices(b, k0, n)).then_inc(load_sem[m % RAWS], 16)

            def load_gu(s_, e):
                for j, src in enumerate((w_exp_gate, w_exp_up)):
                    sp.dma_start(w_gu[s_][:, :, j, :],
                                 src[0, e].rearrange("o (k p) n -> p (o k) n", p=P)).then_inc(gu_load[s_], 16)

            def load_dn(s_, e):
                sp.dma_start(w_dn[s_][:], w_exp_down[0, e].rearrange("o (k p) n -> p (o k) n", p=P)
                             ).then_inc(dn_load[s_], 16)

            for m, (b, k0, n) in enumerate(loads):
                load(m)
                if k0 + n < blocks[b][2]:
                    continue
                if b == last["wb"]:
                    sp.wait_ge(ds_done, NC - 1)
                    sp.dma_start(x_again[:], x[0].rearrange("(t q) d -> q t d", q=P)).then_inc(x2_loaded, 16)
                if b == last["wa"]:
                    sp.wait_ge(ya_made, NC)
                    sp.dma_start(ln1g[:], ln1_g[0:1].to_broadcast([P, D])).then_inc(ln1_loaded, 16)
                    sp.dma_start(ln1b[:], ln1_b[0:1].to_broadcast([P, D])).then_inc(ln1_loaded, 16)
                    sp.dma_start(p_tok[:], p[0, 0].rearrange("(t q) d -> q t d", q=P)).then_inc(p_loaded, 16)
                if b == last["wo"]:
                    sp.wait_ge(block_read, last["wa"] + 1)
                    sp.dma_start(pleb[:], b_ple_gate[0:1].to_broadcast([P, D])).then_inc(pleb_loaded, 16)
                    sp.wait_ge(block_done, last["wa"] + 1)
                    load_gu(0, bass.ds(0, 1))
                if b == last["rt"]:
                    sp.wait_ge(merged_ready, 2)
                    load_gu(1, bass.ds(1, 1))
                if b == last["pg"]:
                    load_gu(2, bass.ds(2, 1))
                    sp.wait_ge(tr_done, 12)
                    load_dn(0, bass.ds(0, 1))
                    load_dn(1, bass.ds(1, 1))
            sp.wait_ge(block_read, last["wo"] + 1)
            sp.dma_start(ln2g[:], ln2_g[0:1].to_broadcast([P, D])).then_inc(ln2_loaded, 16)
            sp.dma_start(ln2b[:], ln2_b[0:1].to_broadcast([P, D])).then_inc(ln2_loaded, 16)
            sp.wait_ge(h_ready, TT)
            load_dn(2, bass.ds(2, 1))
            sp.wait_ge(lo_ready, len(slices))
            load_gu(3, bass.ds(3, 1))
            load_dn(3, bass.ds(3, 1))

            def quad_loads(r, i):
                for par in range(2):
                    for s_ in (2 * par, 2 * par + 1):
                        sp.wait_ge(gu_done, 32 * r + 4 * i + s_ - 3)
                        load_gu(s_, bass.ds(4 * i + s_, 1))
                    sp.wait_ge(dn_done, 32 * r + 4 * i + 2 * par - 2)
                    for s_ in (2 * par, 2 * par + 1):
                        load_dn(s_, bass.ds(4 * i + s_, 1))

            with sp.Fori(1, N_EXP // 4) as i:
                quad_loads(0, i)
            sp.wait_ge(rt_done, 1)
            again = sp.value_load(more[0:1, 0:1])
            with sp.If(again > 0):
                with sp.Fori(1, PASSES) as r:
                    with sp.Fori(0, N_EXP // 4) as i:
                        quad_loads(r, i)
            for t in range(TT):
                sp.wait_ge(h_ready, TT + t + 1)
                sp.dma_start(out[0, t * P:(t + 1) * P, :], h_tok[:, t, :]).then_inc(stored, 16)
            sp.wait_ge(stored, 16 * TT)

        @block.tensor
        def _(pe):
            mm, tr = nc.tensor.matmul, nc.tensor.transpose
            at_slice = [0]

            def slices_pe(n):
                for _ in range(n):
                    j = at_slice[0]
                    at_slice[0] += 1
                    b, kt = slices[j]
                    name, act_pair, kts, _, wd = blocks[b]
                    a_hi, a_lo = pairs[act_pair]
                    if kt == 0:
                        if b >= 2:
                            pe.wait_ge(block_read, b - 1)
                        if act_pair == "ya":
                            pe.wait_ge(ya_made, NC)
                        elif act_pair == "p":
                            pe.wait_ge(p_made, 1)
                        else:
                            pe.wait_ge(lo_made, lo_needed[act_pair])
                    pe.wait_ge(lo_ready, j + 1)
                    hi, lo = w_hi[:, j % RING, :], w_lo[:, j % RING, :]
                    cols = dbank[:, (b % 2) * 1024:(b % 2) * 1024 + 1024]
                    parts = ((a_hi, hi), (a_lo, hi), (a_hi, lo))
                    outs = []
                    if name in ("k", "q", "v", "qa"):
                        outs = [(cols[:, c * T:(c + 1) * T], c * P, None) for c in range(4)]
                    elif name == "kva":
                        outs = [(cols[:, c * T:(c + 1) * T], c * P, None) for c in range(2)]
                        outs += [(cols[:, 512 + t * 256:768 + t * 256], 256, t) for t in range(TT)]
                    else:
                        outs = [(cols[:, t * 512:t * 512 + wd], 0, t) for t in range(TT)]
                    seen = set()
                    for o, c0, t in outs:
                        bank = c0 // 256 if t is None else ("b" if name == "kva" else t)
                        for q, (a, w_) in enumerate(parts):
                            begin = kt == 0 and q == 0 and bank not in seen
                            seen.add(bank)
                            end = kt == kts - 1 and q == 2
                            if t is None:
                                ins = mm(o, w_[:, c0:c0 + P], a[:, kt, :], start=begin, stop=end, skip_group_check=True)
                            else:
                                ins = mm(o, a[:, kt, t * P:(t + 1) * P], w_[:, c0:wd], start=begin, stop=end,
                                         skip_group_check=True)
                    if kt == kts - 1:
                        ins.then_inc(block_done, 1)
                        pe.wait_ge(block_done, b + 1)
                        pe.nop().then_inc(slice_used, 1)
                    else:
                        ins.then_inc(slice_used, 1)

            def turn_tokens(src, banks=4):
                for q in range(banks):
                    for k in range(2):
                        for t in range(TT):
                            ins = tr(xbank[:, q * 512 + k * T + t * P:q * 512 + k * T + (t + 1) * P],
                                     src[:, t, (2 * q + k) * P:(2 * q + k + 1) * P], ident[:])
                    ins.then_inc(tr_done, 1)

            pe.wait_ge(ident_ready, 1)
            pe.wait_ge(x_loaded, 16)
            turn_tokens(x_tok)
            pe.wait_ge(small_loaded, 16 * 5)
            pe.wait_ge(lo_made, 1)
            tr(xbank[:, 0:TAPS * 24], conv_rows[0:TAPS * 24, :], ident[0:TAPS * 24, 0:TAPS * 24]).then_inc(cw_tr, 1)
            slices_pe(8 + 12)
            pe.wait_ge(ab3, 1)
            pe.wait_ge(cw_ready, 1)
            pe.wait_ge(consts, 1)
            for t in range(TT):
                mm(xbank[:, t * H:(t + 1) * H], tri[:], decay_g[:, t, :], start=True, stop=True)
                mm(xbank[:, 16 + t * H:16 + (t + 1) * H], chunk1[:], decay_g[:, t, :], start=True, stop=True)
                for b in range(2):
                    ins = mm(xbank[:, 32 + (2 * t + b) * H:40 + (2 * t + b) * H], half_rows[:, b, :], decay_g[:, t, :],
                             start=True, stop=True)
            ins.then_inc(cum_done, 1)

            def norm_sums(n):
                pe.wait_ge(squared, n + 1)
                if n == 0:
                    pe.wait_ge(cum_read, 1)
                if n >= 2:
                    pe.wait_ge(rs_ready, n - 1)
                for hh in range(2):
                    o0 = (n % 2) * 1024 + hh * 512
                    ins = mm(xbank[:, o0:o0 + 512], ones[:], sq[:, 2 * hh:2 * hh + 2, :], start=True, stop=True)
                ins.then_inc(sq_summed, 1)

            slices_pe(12)
            norm_sums(0)
            slices_pe(8)
            norm_sums(1)
            slices_pe(8)
            norm_sums(2)
            slices_pe(8)
            norm_sums(3)
            slices_pe(4)
            pe.wait_ge(beta_ready, 1)
            pe.wait_ge(rs_ready, 4)
            for h in range(H):
                for t in range(TT):
                    ins = mm(xbank[:, h * T + t * P:h * T + (t + 1) * P], bc(beta[:, t, h:h + 1], [P, P]), ident[:],
                             start=True, stop=True)
            ins.then_inc(brow, 1)
            slices_pe(4)
            pe.wait_ge(kb_ready, 1)
            for h in range(H):
                for t in range(TT):
                    ins = mm(xbank[:, h * T + t * P:h * T + (t + 1) * P], bc(decay_g[:, t, h:h + 1], [P, P]), tri[:],
                             start=True, stop=True)
            ins.then_inc(grow, 1)
            slices_pe(4)

            def gram_of(left, right, bank0):
                for h in range(H):
                    for t in range(TT):
                        for b in range(2):
                            tk = t * P + b * C
                            o0 = bank0 * 512 + (h * TT + t) * C
                            ins = mm(xbank[b * C:(b + 1) * C, o0:o0 + C], left[:, h, tk:tk + C], right[:, h, tk:tk + C],
                                     start=True, stop=True)
                ins.then_inc(gram, 1)

            pe.wait_ge(dec_raw, 1)
            gram_of(kT, kbT, 0)
            gram_of(kbT, kT, 2)
            slices_pe(2)
            pe.wait_ge(gram_read, 1)
            gram_of(kT, qT, 0)
            slices_pe(2)
            pe.wait_ge(conv_out, 6)
            pe.wait_ge(gram_read, 3)
            for src, done in ((vT, vtr), (kT, ktr)):
                for t in range(TT):
                    for h in range(H):
                        ins = tr(xbank[:, t * D + h * P:t * D + (h + 1) * P], src[:, h, t * P:(t + 1) * P], ident[:])
                    ins.then_inc(done, 1)
                slices_pe(2)
                if src is vT:
                    pe.wait_ge(vb_ready, TT)
            pe.wait_ge(kdec_ready, TT)

            def unit_products(bank0, left, right):
                for u in range(U):
                    for b in range(2):
                        rows = slice(b * C, (b + 1) * C)
                        o0 = bank0 * 512 + u * C
                        ins = mm(xbank[rows, o0:o0 + C], left[rows, u, :], right[rows, u, :], start=True, stop=True)
                return ins

            for lev in range(1, 6):
                pe.wait_ge(lev_masked, lev)
                pe.wait_ge(inv_ready, 2 * lev)
                unit_products(0, LT_lev[:, lev % 2], inv).then_inc(lev_prod, 1)
                slices_pe(2)
                pe.wait_ge(lev_copied, lev)
                if lev < 5:
                    unit_products(2, invT, prod).then_inc(lev_join, 1)
                unit_products(0, prod, invT).then_inc(lev_join, 1)
                slices_pe(2)

            def scan_a(n):
                t, b = n // 2, n % 2
                rows = slice(b * C, (b + 1) * C)
                tok = slice(n * C, (n + 1) * C)
                if n == 0:
                    pe.wait_ge(inv_ready, 11)
                    pe.wait_ge(eg_used, 2)
                else:
                    pe.wait_ge(s_ready, n)
                    pe.wait_ge(o_read, n)
                    for h in range(H):
                        ins = mm(xbank[rows, h * P:(h + 1) * P], kbT[:, h, tok], S[:, h, :], start=True, stop=True)
                    ins.then_inc(ks_done, 1)
                    for h in range(H):
                        ins = mm(xbank[rows, 1024 + h * P:1024 + (h + 1) * P], qT[:, h, tok], S[:, h, :],
                                 start=h % 4 == 0, stop=False, skip_group_check=True)
                    ins.then_inc(ks_done, 1)

            def scan_b(n):
                t, b = n // 2, n % 2
                rows = slice(b * C, (b + 1) * C)
                if n > 0:
                    pe.wait_ge(r_ready, n)
                for h in range(H):
                    rhs = vb[rows, t, h * P:(h + 1) * P] if n == 0 else R[rows, h * P:(h + 1) * P]
                    ins = mm(xbank[rows, h * P:(h + 1) * P], invT[rows, h * TT + t, :], rhs, start=True, stop=True)
                ins.then_inc(vn_done, 1)

            def scan_c(n):
                t, b = n // 2, n % 2
                rows = slice(b * C, (b + 1) * C)
                pe.wait_ge(vn_ready, n + 1)
                if n < NC - 1:
                    for h in range(H):
                        ins = mm(xbank[:, h * P:(h + 1) * P], kdec[rows, t, h * P:(h + 1) * P],
                                 v_new[rows, h * P:(h + 1) * P], start=True, stop=True)
                    ins.then_inc(ds_done, 1)
                for h in range(H):
                    ins = mm(xbank[rows, 1024 + h * P:1024 + (h + 1) * P], attT[rows, h * TT + t, :],
                             v_new[rows, h * P:(h + 1) * P], start=(n == 0 and h % 4 == 0), stop=True,
                             skip_group_check=True)
                ins.then_inc(o_done, 1)

            for n in range(NC):
                scan_a(n)
                slices_pe(1)
                scan_b(n)
                slices_pe(1)
                scan_c(n)
                slices_pe(1)

            def att_scores(c):
                if c == 0:
                    pe.wait_ge(block_read, kv_b + 1)
                    pe.wait_ge(o_read, NC)
                elif c == 1:
                    pe.wait_ge(lo_made, 8)
                else:
                    pe.wait_ge(ya_made, c)
                for hp in range(HP):
                    g = hp // 2
                    for hh in range(2):
                        rows = slice(hh * C, (hh + 1) * C)
                        q_ = qaT[rows, hp, c * C:(c + 1) * C]
                        o = xbank[rows, hp * P:(hp + 1) * P]
                        if c == 0:
                            ins = mm(o[:, 0:C], q_, kaT[rows, g, 0:C], start=True, stop=True)
                        elif c % 2:
                            ins = mm(o, q_, kaT[rows, g, (c - 1) * C:(c + 1) * C], start=True, stop=True)
                        else:
                            mm(o[:, 0:C], q_, kaT[rows, g, c * C:(c + 1) * C], start=True, stop=True)
                            ins = mm(o[:, C:P], q_, kaT[rows, g, (c - 1) * C:c * C], start=True, stop=True)
                ins.then_inc(sc_done, 1)

            def att_turn(c):
                kk = C if c == 0 else P
                pe.wait_ge(pr_ready, c + 1)
                for hp in range(HP):
                    ins = tr(xbank[0:kk, 1024 + hp * P:1024 + (hp + 1) * P], pr[:, hp, 0:kk], ident[:])
                ins.then_inc(pt_done, 1)

            def att_pv(c):
                kk = C if c == 0 else P
                vt = (0, 0, 2, 1)[c]
                pe.wait_ge(pt_read, c + 1)
                for g in range(KVH):
                    for hh in range(2):
                        rows = slice(hh * C, (hh + 1) * C)
                        ins = mm(xbank[rows, 2 * g * C:(2 * g + 2) * C], va[0:kk, vt, g * C:(g + 1) * C],
                                 prT[0:kk, 2 * g:2 * g + 2, hh * C:(hh + 1) * C], start=True, stop=True)
                ins.then_inc(pv_done, 1)

            for c in range(NC):
                att_scores(c)
                slices_pe(ATT_SLICES[c][0])
                att_turn(c)
                slices_pe(ATT_SLICES[c][1])
                att_pv(c)
                slices_pe(ATT_SLICES[c][2])
                if c == 0:
                    slices_pe(3)
                    pe.wait_ge(ya_made, 1)
                    pe.wait_ge(o_final, TT)
                    turn_tokens(o_tok)
                    slices_pe(2)
            slices_pe(first_slice[last["wa"] + 1] - at_slice[0])
            pe.wait_ge(ya_made, NC)
            pe.wait_ge(p_loaded, 16)
            for k in range(2):
                for t in range(TT):
                    ins = tr(xbank[:, k * T + t * P:k * T + (t + 1) * P], p_tok[:, t, k * P:(k + 1) * P], ident[:])
            ins.then_inc(p_turned, 1)
            pe.wait_ge(p_made, 1)
            pe.wait_ge(merged_ready, 2)
            turn_tokens(merged)
            slices_pe(first_slice[last["wo"] + 1] - at_slice[0])
            pe.wait_ge(h_ready, TT)
            turn_tokens(h_tok)
            slices_pe(8)
            slices_pe(4)
            pe.wait_ge(rt_picked, 1)
            pe.wait_ge(lo_made, 16)
            mm(xbank[:, 0:N_EXP], before[:], picked[:, 0, :], start=True, stop=True)
            mm(xbank[:, N_EXP:2 * N_EXP], ones[:], picked[:, 0, :], start=True, stop=False, skip_group_check=True)
            mm(xbank[:, N_EXP:2 * N_EXP], before[:], picked[:, 1, :], start=False, stop=True, skip_group_check=True)
            mm(xbank[:, 2 * N_EXP:3 * N_EXP], ones[:], picked[:, 0, :], start=True, stop=False, skip_group_check=True)
            mm(xbank[:, 2 * N_EXP:3 * N_EXP], ones[:], picked[:, 1, :], start=False, stop=True,
               skip_group_check=True).then_inc(rt_cum, 1)
            slices_pe(len(slices) - at_slice[0])
            pe.wait_ge(rt_done, 1)
            pe.wait_ge(block_read, len(blocks))
            pe.wait_ge(hk_ready, TT)

            def gather(g, half):
                if half == 0:
                    pe.wait_ge(sel_ready, g + 1)
                for k in range(4 * half, 4 * half + 4):
                    for t in range(TT):
                        for part in (hk_hi, hk_lo):
                            ins = mm(dbank[:, k * P:(k + 1) * P], part[:, t, k * P:(k + 1) * P], sel[:, t, :],
                                     start=(k % 4 == 0 and t == 0 and part is hk_hi), stop=(t == 1 and part is hk_lo),
                                     skip_group_check=True)
                ins.then_inc(gather_done, 1)

            def turn_sel(e):
                for t in range(TT):
                    tr(psD[:, 2, t * P:(t + 1) * P], sel[:, t, :].bitcast(F32), ident[:])
                for t in range(TT):
                    ins = mm(psD[:, 2, 256:258], sel[:, t, :].bitcast(F32), comb[:, t, e], start=t == 0, stop=t == 1,
                             skip_group_check=True)
                ins.then_inc(selt_done, 1)

            def scatter(m, par, hf):
                pe.wait_ge(ylo_ready, 2 * m + hf + 1)
                for t in range(TT):
                    if hf:
                        pe.wait_ge(acc_added, 4 * m + 2 + t)
                    for part in (y_hi, y_lo):
                        ins = mm(psX[:, t, :], selT[:, par, t, :], part[:, hf * W:(hf + 1) * W],
                                 start=part is y_hi, stop=part is y_lo)
                    ins.then_inc(sc_out, 1)

            def expert_pair(r, i, par, first=False):
                n = 16 * r + 2 * i + par
                g = 17 * r + 2 * i + par
                pe.wait_ge(gath_ready, 2 * g + 2)
                pe.wait_ge(selt_ready, g + 1)
                for a in range(2):
                    pe.wait_ge(gu_load[2 * par + a], 256 * r + 32 * i + 32)
                    for k in range(KT):
                        rows = slice((k % 2) * C, (k % 2 + 1) * C)
                        ins = mm(psD[rows, 2 + a, :], gath[:, k, a * C:(a + 1) * C],
                                 w_gu[2 * par + a][:, k].rearrange("p j n -> p (j n)"), start=k < 2, stop=k >= KT - 2,
                                 skip_group_check=True)
                    ins.then_inc(gu_done, 1)
                    if not first:
                        scatter(n - 1, 1 - par, a)
                gather(g + 1, 0)
                for a in range(2):
                    pe.wait_ge(gus_ready, 2 * n + a + 1)
                    if a == 0:
                        pe.wait_ge(acc_added, 4 * n + 1)
                    for q in range(4):
                        ins = mm(psX[:, a, q * C:(q + 1) * C], gus[:, a, q * P:(q + 1) * P], stack_eye[:],
                                 start=True, stop=True)
                    ins.then_inc(t_done, 1)
                gather(g + 1, 1)
                turn_sel(bass.ds(4 * i + 2 * par + 2, 2))
                pe.wait_ge(he_ready, 2 * n + 2)
                for hf in range(2):
                    for k in range(2):
                        for a in range(2):
                            if hf == 0 and k == 0:
                                pe.wait_ge(dn_load[2 * par + a], 128 * r + 16 * i + 16)
                            ins = mm(psX[a * C:(a + 1) * C, 2 + hf, :], he[:, a, k, :],
                                     w_dn[2 * par + a][:, k, hf * W:(hf + 1) * W], start=k == 0, stop=k == 1,
                                     skip_group_check=True)
                    ins.then_inc(dn_done, 1)

            def expert_pass(r):
                if not isinstance(r, int):
                    pe.wait_ge(gath_ready, 34 * r)
                    pe.wait_ge(selt_ready, 17 * r)
                gather(17 * r, 0)
                gather(17 * r, 1)
                turn_sel(slice(0, 2))
                expert_pair(r, 0, 0, first=True)
                expert_pair(r, 0, 1)
                with pe.Fori(1, N_EXP // 4) as i:
                    for par in range(2):
                        expert_pair(r, i, par)
                for hf in range(2):
                    scatter(16 * r + 15, 1, hf)

            expert_pass(0)
            again = pe.value_load(more[0:1, 0:1])
            with pe.If(again > 0):
                with pe.Fori(1, PASSES) as r:
                    expert_pass(r)

        @block.scalar
        def _(act):
            link, settle = chain(act, act_s)
            fn = nc.scalar.activation
            at_slice = [0]
            for dst, src in ((alog, a_log), (dtb, dt_bias)):
                act.dma_start(dst[:], src[0:1].to_broadcast([P, H])).then_inc(small_loaded, 16)
            act.dma_start(norm_g[:], gdn_norm_g[0:1].to_broadcast([P, P])).then_inc(small_loaded, 16)
            act.dma_start(conv_rows[0:TAPS * 24, :], conv_w[0].rearrange("k (c q) -> (k c) q", q=P)
                          ).then_inc(small_loaded, 16)
            act.dma_start(sink_all[:], attn_sink[0:1].to_broadcast([P, 2 * HP])).then_inc(small_loaded, 16)
            act.dma_start(rt_b[:, 0:N_GRP], b_route_group[0:1].to_broadcast([P, N_GRP])).then_inc(bias_loaded, 16)
            act.dma_start(rt_b[:, N_GRP:], b_route_expert[0:1].to_broadcast([P, N_EXP])).then_inc(bias_loaded, 16)

            def evacuate(b):
                name, _, _, off, wd = blocks[b]
                n = b - names.index(name)
                cols = dbank[:, (b % 2) * 1024:(b % 2) * 1024 + 1024]
                chan = cols.rearrange("p (c t) -> p c t", c=4)
                tok = cols.rearrange("p (t n) -> p t n", t=TT)
                if name in ("ab", "k", "q", "v", "qa", "kva", "z", "ga", "gb"):
                    act.wait_ge(block_done, b + 1)
                if name == "ab":
                    fn(ab[:], tok[:, :, 0:16], ACT.Copy).then_inc(block_read, 1)
                elif name in ("k", "q", "v"):
                    if b >= 3:
                        act.wait_ge(conv_ready, b - 2)
                    fn(conv_in[:, b % 2, :, TAPS - 1:], chan, ACT.Copy).then_inc(block_read, 1)
                elif name == "qa":
                    fn(qaT[:, 4 * n:4 * n + 4, :], chan, ACT.Copy, scale=0.125).then_inc(block_read, 1)
                elif name == "kva":
                    for hs in range(2):
                        for hh in range(2):
                            fn(kaT[hh * C:(hh + 1) * C].rearrange("p (c s) t -> p s c t", s=2)[:, hs],
                               chan[hs * C:(hs + 1) * C, 0:2, :], ACT.Copy)
                    fn(va[:, 0:2, :], chan[:, 2:4, :], ACT.Copy)
                    fn(va[0:C, 2, :], chan[0:C, 3, :], ACT.Copy)
                    link(fn(va[C:P, 2, :], chan[C:P, 2, :], ACT.Copy))
                    settle()
                    act.nop().then_inc(block_read, 1)
                elif name == "z":
                    if n == 0:
                        act.wait_ge(conv_out, 6)
                    fn(zg[:, :, n * W:(n + 1) * W], tok, ACT.Tanh, scale=0.5).then_inc(z_th, 1)
                elif name in ("ga", "gb"):
                    if name == "ga" and n == 0:
                        act.wait_ge(eg_used, 2)
                    if name == "gb" and n == 0:
                        act.wait_ge(o_summed, 1)
                    fn((th_a if name == "ga" else th_b)[:, :, n * W:(n + 1) * W], tok, ACT.Tanh,
                       scale=0.5).then_inc(block_read, 1)

            def finish(b):
                name = names[b]
                if name in ("k", "q", "v"):
                    act.wait_ge(conv_ready, b)
                    fn(conv_t[:], conv_y[:], ACT.Tanh, scale=0.5).then_inc(conv_th, 1)
                elif name == "pg":
                    n = b - names.index(name)
                    act.wait_ge(pg_in, n + 1)
                    fn(th_p[:, :, n * W:(n + 1) * W], th_p[:, :, n * W:(n + 1) * W], ACT.Tanh,
                       scale=0.5).then_inc(pg_th, 1)

            def slices_act(n):
                for _ in range(n):
                    j = at_slice[0]
                    at_slice[0] += 1
                    if j < len(slices):
                        m, q = place[j]
                        wd = blocks[slices[j][0]][4]
                        if q == 0:
                            act.wait_ge(load_sem[m % RAWS], load_count(m))
                        if j >= RING:
                            act.wait_ge(slice_used, j - RING + 1)
                        fn(w_hi[:, j % RING, 0:wd], raw[:, m % RAWS, q, 0:wd], ACT.Copy).then_inc(hi_ready, 1)
                    if j - LEAD in end_slice:
                        evacuate(end_slice[j - LEAD])
                    if j - LEAD - 4 in end_slice:
                        finish(end_slice[j - LEAD - 4])

            def pair_hi(name, n):
                hi = pairs[name][0]
                for q in range(4):
                    act.wait_ge(tr_done, 4 * n + q + 1)
                    fn(hi[:, 2 * q:2 * q + 2, :], psX[:, q, :].rearrange("p (k t) -> p k t", k=2),
                       ACT.Copy).then_inc(hi_made, 1)

            slices_act(LEAD)
            pair_hi("x", 0)
            act.wait_ge(cw_tr, 1)
            fn(conv_c[:], xbank[:, 0:TAPS * 24].rearrange("p (k c) -> p k c", k=TAPS), ACT.Copy).then_inc(cw_ready, 1)
            act.wait_ge(small_loaded, 16 * 5)
            by_half = sink_all[:].rearrange("p (q two) -> p two q", two=2)
            for hh in range(2):
                ins = fn(sink[hh * C:(hh + 1) * C, :], by_half[hh * C:(hh + 1) * C, hh, :], ACT.Copy)
            ins.then_inc(sink_ready, 1)
            act.wait_ge(biases_ready, 1)
            slices_act(8)
            act.wait_ge(ab1, 1)
            link(fn(softb[:], softb[:], ACT.Exp, scale=-1.0))
            settle()
            fn(softb[:], softb[:], ACT.Ln, bias=one[:, 0:1])
            fn(neg_a[:], alog[:], ACT.Exp)
            fn(beta[:], ab[:, :, 0:H], ACT.Exp, scale=-1.0).then_inc(ab2, 1)
            slices_act(12)
            act.wait_ge(cum_read, 1)
            fn(to_end[:], to_end[:], ACT.Exp)
            fn(g_chunk[:], g_chunk[:], ACT.Exp).then_inc(cum_exp, 1)

            def norm_rs(n):
                act.wait_ge(sq_summed, n + 1)
                if n >= 2:
                    act.wait_ge(normed, n - 1)
                src = xbank[:, (n % 2) * 1024:(n % 2) * 1024 + 1024].rearrange("p (c t) -> p c t", c=4)
                link(fn(rs[:, n % 2], src, ACT.Ln, bias=eps_l2[:, 0:1]))
                settle()
                fn(rs[:, n % 2], rs[:, n % 2], ACT.Exp, scale=-0.5).then_inc(rs_ready, 1)

            slices_act(12)
            norm_rs(0)
            slices_act(8)
            norm_rs(1)
            slices_act(8)
            norm_rs(2)
            slices_act(8)
            norm_rs(3)
            slices_act(4)
            slices_act(4)
            act.wait_ge(grow, 1)
            act.wait_ge(z_free, 1)
            fn(eg[:], xbank[:].rearrange("p (h t) -> p h t", h=H), ACT.Exp).then_inc(eg_ready, 1)
            slices_act(4)
            act.wait_ge(dec_masked, 2)
            fn(dec_sub[:], dec_sub[:], ACT.Exp)
            fn(dec_up[:], dec_up[:], ACT.Exp).then_inc(dec_ready, 1)
            slices_act(2)
            slices_act(2)
            slices_act(2)
            slices_act(2)
            for lev in range(1, 6):
                act.wait_ge(lev_prod, lev)
                fn(prod[:], xbank[:, 0:1024].rearrange("p (u c) -> p u c", u=U), ACT.Copy).then_inc(lev_copied, 1)
                slices_act(4)
            for n in range(NC):
                t, b = n // 2, n % 2
                rows = slice(b * C, (b + 1) * C)
                slices_act(1)
                act.wait_ge(vn_done, n + 1)
                fn(v_new[rows, :], xbank[rows, 0:1024], ACT.Copy).then_inc(vn_ready, 1)
                slices_act(1)
                act.wait_ge(o_done, n + 1)
                fn(o_tok[rows, t, :], xbank[rows, 1024:2048], ACT.Copy).then_inc(o_read, 1)
                slices_act(1)
            for c in range(NC):
                kk = C if c == 0 else P
                act.wait_ge(sc_shift, c + 1)
                fn(sexp[:, 0, :], sexp[:, 0, :], ACT.Exp)
                fn(pr[:, :, 0:kk], pr[:, :, 0:kk], ACT.Exp).then_inc(sc_exp, 1)
                slices_act(ATT_SLICES[c][0])
                act.wait_ge(pt_done, c + 1)
                fn(prT[0:kk], xbank[0:kk, 1024:2048].rearrange("p (c t) -> p c t", c=HP), ACT.Copy).then_inc(pt_read, 1)
                slices_act(ATT_SLICES[c][1])
                act.wait_ge(pv_done, c + 1)
                fn(pairs["ya"][0][:, :, c * C:(c + 1) * C], xbank[:, 0:512].rearrange("p (c t) -> p c t", c=HP),
                   ACT.Copy).then_inc(ya_hi, 1)
                slices_act(ATT_SLICES[c][2])
                if c == 0:
                    act.wait_ge(o_summed, 1)
                    link(fn(o_rs[:], o_sum[:], ACT.Ln, scale=1.0 / P, bias=eps_norm[:, 0:1]))
                    settle()
                    fn(o_rs[:], o_rs[:], ACT.Exp, scale=-0.5).then_inc(o_rs_ready, 1)
                    slices_act(3)
                    pair_hi("yb", 1)
                    slices_act(2)
            slices_act(first_slice[last["wa"] + 1] + LEAD - at_slice[0])
            act.wait_ge(p_turned, 1)
            fn(pairs["p"][0][:], psX[:, 0, :].rearrange("p (k t) -> p k t", k=2), ACT.Copy).then_inc(p_hi, 1)
            pair_hi("m", 2)
            slices_act(first_slice[last["wo"] + 1] + LEAD - at_slice[0])

            def norm_rstd(n):
                act.wait_ge(ln_var, n + 1)
                link(fn(rstd[:], mv[:, :, 1], ACT.Ln, bias=eps_ln[:, 0:1]))
                settle()
                fn(rstd[:], rstd[:], ACT.Exp, scale=-0.5).then_inc(ln_rstd, 1)

            norm_rstd(0)
            for t in range(TT):
                act.wait_ge(h_ready, t + 1)
            pair_hi("h", 3)
            slices_act(8)
            act.wait_ge(rt_in, 1)
            fn(g8[:, :, 0:N_GRP], g8[:, :, 0:N_GRP], ACT.Exp)
            fn(r_small[:, 0, :], r_small[:, 0, :], ACT.Exp).then_inc(rt_exp, 1)
            slices_act(4)
            slices_act(len(slices) + LEAD + 5 - at_slice[0])
            act.wait_ge(slice_used, len(slices))
            act.wait_ge(h_ready, TT)
            for t in range(TT):
                fn(hk_hi[:, t, :], h_tok[:, t, :], ACT.Copy).then_inc(hk_hi_ready, 1)

            def take_gather(g, half):
                act.wait_ge(gather_done, 2 * g + half + 1)
                fn(gath[:, 4 * half:4 * half + 4, :], psD[:, half, :].rearrange("p (k s) -> p k s", k=4),
                   ACT.Copy).then_inc(gath_ready, 1)

            def take_sel(g, par):
                act.wait_ge(selt_done, g + 1)
                fn(selT[:, par], psD[:, 2, 0:256].rearrange("p (t s) -> p t s", t=TT), ACT.Copy)
                for a in range(2):
                    ins = fn(w_slot[a * C:(a + 1) * C, par:par + 1], psD[a * C:(a + 1) * C, 2, 256 + a:257 + a], ACT.Copy)
                ins.then_inc(selt_ready, 1)

            def expert_pass(r):
                take_gather(17 * r, 0)
                take_gather(17 * r, 1)
                take_sel(17 * r, 0)
                with act.Fori(0, N_EXP // 4) as i:
                    for par in range(2):
                        n = 16 * r + 2 * i + par
                        g = 17 * r + 2 * i + par
                        take_gather(g + 1, 0)
                        for a in range(2):
                            act.wait_ge(t_done, 2 * n + a + 1)
                            fn(sg[:, a], psX[:, a, 0:2 * C].rearrange("p (k s) -> p k s", k=2), ACT.Silu
                               ).then_inc(silu_done, 1)
                        take_gather(g + 1, 1)
                        take_sel(g + 1, 1 - par)
                        for hf in range(2):
                            act.wait_ge(dn_done, 2 * n + hf + 1)
                            fn(y_hi[:, hf * W:(hf + 1) * W], psX[:, 2 + hf, :], ACT.Copy,
                               scale=w_slot[:, par:par + 1]).then_inc(yhi_ready, 1)

            expert_pass(0)
            act.wait_ge(rt_done, 1)
            again = act.value_load(more[0:1, 0:1])
            with act.If(again > 0):
                with act.Fori(1, PASSES) as r:
                    expert_pass(r)
            norm_rstd(1)

        @block.vector
        def _(dve):
            v = nc.vector
            link, settle = chain(dve, vec)
            at_slice = [0]

            def evacuate(b):
                name, _, _, off, wd = blocks[b]
                n = b - names.index(name)
                cols = dbank[:, (b % 2) * 1024:(b % 2) * 1024 + 1024]
                tok = cols.rearrange("p (t n) -> p t n", t=TT)
                c0 = n * W
                if name in ("k", "q", "v"):
                    if b == 1:
                        dve.wait_ge(cw_ready, 1)
                    dve.wait_ge(block_read, b + 1)
                    if b > 1:
                        dve.wait_ge(conv_out, b - 1)
                    xin = conv_in[:, b % 2]
                    ct0 = {"q": 0, "k": 8, "v": 16}[name] + 4 * n
                    for tap in range(TAPS):
                        for c in range(4):
                            wt = conv_c[:, tap, ct0 + c:ct0 + c + 1]
                            src = xin[:, c, tap:tap + T]
                            if tap == 0:
                                ins = link(v.tensor_scalar(conv_y[:, c, :], src, wt, None, ALU.mult))
                            else:
                                ins = v.scalar_tensor_tensor(conv_y[:, c, :], src, wt, conv_y[:, c, :], ALU.mult, ALU.add)
                                if tap < TAPS - 1:
                                    link(ins)
                        if tap < TAPS - 1:
                            settle()
                    ins.then_inc(conv_ready, 1)
                elif name == "z":
                    dve.wait_ge(z_th, n + 1)
                    v.scalar_tensor_tensor(zg[:, :, c0:c0 + W], zg[:, :, c0:c0 + W], 1.0, tok, ALU.add, ALU.mult
                                           ).then_inc(block_read, 1)
                elif name == "wb":
                    dve.wait_ge(block_done, b + 1)
                    dve.wait_ge(block_read, last["gb"] + 1)
                    v.scalar_tensor_tensor(merged[:, :, c0:c0 + W], th_b[:, :, c0:c0 + W], 1.0, tok, ALU.add, ALU.mult
                                           ).then_inc(block_read, 1)
                elif name == "wa":
                    dve.wait_ge(block_done, b + 1)
                    if n:
                        dve.wait_ge(merged_ready, n)
                    v.scalar_tensor_tensor(gated_a[:], th_a[:, :, c0:c0 + W], 1.0, tok, ALU.add, ALU.mult
                                           ).then_inc(block_read, 1)
                elif name == "wo":
                    dve.wait_ge(block_done, b + 1)
                    dve.wait_ge(ax_ready, 1)
                    v.scalar_tensor_tensor(h_tok[:, :, c0:c0 + W], tok, 0.5, x_again[:, :, c0:c0 + W], ALU.mult, ALU.add
                                           ).then_inc(block_read, 1)
                elif name == "rt":
                    dve.wait_ge(block_done, b + 1)
                    dve.wait_ge(bias_loaded, 32)
                    for t in range(TT):
                        ins = v.tensor_tensor(lg[:, t, :], tok[:, t, 0:wd], rt_b[:], ALU.add)
                        if t == 0:
                            link(ins)
                    ins.then_inc(block_read, 1)
                elif name == "pg":
                    dve.wait_ge(block_done, b + 1)
                    dve.wait_ge(pleb_loaded, 16)
                    for t in range(TT):
                        ins = v.tensor_tensor(th_p[:, t, c0:c0 + W], tok[:, t, :], pleb[:, c0:c0 + W], ALU.add)
                    ins.then_inc(block_read, 1)
                    dve.wait_ge(block_read, b + 1)
                    v.engine_nop().then_inc(pg_in, 1)
                elif name == "pp":
                    dve.wait_ge(block_done, b + 1)
                    dve.wait_ge(pg_th, n + 1)
                    v.scalar_tensor_tensor(th_p[:, :, c0:c0 + W], th_p[:, :, c0:c0 + W], 1.0, tok, ALU.add, ALU.mult
                                           ).then_inc(block_read, 1)

            def finish(b):
                name = names[b]
                n = b - names.index(name)
                if name in ("k", "q", "v"):
                    dst = {"k": kT, "q": qT, "v": vT}[name]
                    dve.wait_ge(conv_th, b)
                    v.scalar_tensor_tensor(dst[:, 4 * n:4 * n + 4, :], conv_t[:], 1.0, conv_y[:], ALU.add, ALU.mult
                                           ).then_inc(conv_out, 1)

            def slices_dve(n):
                for _ in range(n):
                    j = at_slice[0]
                    at_slice[0] += 1
                    if j < len(slices):
                        m, q = place[j]
                        wd = blocks[slices[j][0]][4]
                        dve.wait_ge(hi_ready, j + 1)
                        v.tensor_tensor(w_lo[:, j % RING, 0:wd], raw[:, m % RAWS, q, 0:wd],
                                        w_hi[:, j % RING, 0:wd].bitcast(F32), ALU.subtract).then_inc(lo_ready, 1)
                    if j - LEAD in end_slice:
                        evacuate(end_slice[j - LEAD])
                    if j - LEAD - 4 in end_slice:
                        finish(end_slice[j - LEAD - 4])

            def pair_lo(name, n):
                hi, lo = pairs[name]
                for q in range(4):
                    dve.wait_ge(hi_made, 4 * n + q + 1)
                    v.tensor_tensor(lo[:, 2 * q:2 * q + 2, :], psX[:, q, :].rearrange("p (k t) -> p k t", k=2),
                                    hi[:, 2 * q:2 * q + 2, :].bitcast(F32), ALU.subtract).then_inc(lo_made, 1)

            slices_dve(LEAD)
            pair_lo("x", 0)
            slices_dve(8)
            dve.wait_ge(block_read, 1)
            dve.wait_ge(small_loaded, 16 * 5)
            link(v.tensor_tensor(soft[:], ab[:, :, H:2 * H], dtb_rows(), ALU.add))
            settle()
            v.scalar_tensor_tensor(softb[:], soft[:], -1.0, soft[:], ALU.mult, ALU.max).then_inc(ab1, 1)
            dve.wait_ge(ab2, 1)
            link(v.scalar_tensor_tensor(soft[:], soft[:], 0.0, softb[:], ALU.max, ALU.add))
            link(v.tensor_scalar(beta[:], beta[:], 1.0, None, ALU.add))
            settle()
            v.scalar_tensor_tensor(decay_g[:], soft[:], -1.0, neg_rows(), ALU.mult, ALU.mult).then_inc(ab3, 1)
            link(v.reciprocal(beta[:], beta[:]))
            settle()
            v.tensor_scalar(beta_half[:], beta[:], 0.5, None, ALU.mult).then_inc(beta_ready, 1)
            slices_dve(12)
            dve.wait_ge(cum_done, 1)
            link(v.tensor_copy(gc[:], xbank[:, 0:16].rearrange("p (t h) -> p t h", t=TT)))
            link(v.tensor_copy(g_chunk[:], xbank[:, 32:64].rearrange("p (n h) -> p n h", n=NC)))
            settle()
            v.tensor_tensor(to_end[:], xbank[:, 16:32].rearrange("p (t h) -> p t h", t=TT), gc[:], ALU.subtract
                            ).then_inc(cum_read, 1)

            def normalise(n):
                dst = (kT if n < 2 else qT)[:, 4 * (n % 2):4 * (n % 2) + 4, :]
                dve.wait_ge(rs_ready, n + 1)
                v.scalar_tensor_tensor(dst, dst, 1.0 if n < 2 else P ** -0.5, rs[:, n % 2], ALU.mult, ALU.mult
                                       ).then_inc(normed, 1)

            slices_dve(12)
            normalise(0)
            slices_dve(8)
            normalise(1)
            slices_dve(8)
            normalise(2)
            slices_dve(8)
            normalise(3)
            slices_dve(4)
            dve.wait_ge(brow, 1)
            dve.wait_ge(normed, 4)
            v.tensor_tensor(kbT[:], kT[:], xbank[:].rearrange("p (h t) -> p h t", h=H), ALU.mult).then_inc(kb_ready, 1)
            slices_dve(4)
            dve.wait_ge(grow, 1)
            dve.wait_ge(eg_ready, 1)
            rows_u = xbank[:].rearrange("p (u two c) -> p two u c", two=2, c=C)
            gcu = gc[:].rearrange("p t h -> p h t")
            for b in range(2):
                rows = slice(b * C, (b + 1) * C)
                gview = gc[rows].rearrange("p t h -> p h t").unsqueeze(3).to_broadcast([C, H, TT, C])
                dview = dec_sub[rows].rearrange("p (h t) c -> p h t c", t=TT)
                rview = xbank[rows, :].rearrange("p (h t two c) -> p two h t c", t=TT, two=2, c=C)[:, b]
                ins = v.tensor_tensor(dview, gview, rview, ALU.subtract)
            ins.then_inc(dec_raw, 1)
            slices_dve(4)
            dve.wait_ge(gram, 1)
            dve.wait_ge(dec_ready, 1)
            uv = lambda b0: xbank[:, b0 * 512:b0 * 512 + 1024].rearrange("p (u c) -> p u c", u=U)
            eye_u = stack_eye[:].unsqueeze(1).to_broadcast([P, U, C])
            v.tensor_tensor(LT[:], uv(0), dec_up[:], ALU.mult).then_inc(gram_read, 1)
            dve.wait_ge(gram, 2)
            v.tensor_tensor(inv[:], uv(2), dec_sub[:], ALU.mult).then_inc(gram_read, 1)
            dve.wait_ge(gram_read, 2)
            v.tensor_tensor(inv[:], eye_u, inv[:], ALU.subtract).then_inc(inv_ready, 1)
            link(v.tensor_tensor(invT[:], LT[:], level_mask[:, 0:1, :].to_broadcast([P, U, C]), ALU.mult))
            settle()
            v.tensor_tensor(invT[:], eye_u, invT[:], ALU.subtract).then_inc(inv_ready, 1)
            slices_dve(2)
            dve.wait_ge(gram, 3)
            v.tensor_tensor(attT[:], uv(0), dec_up[:], ALU.mult).then_inc(gram_read, 1)
            slices_dve(2)
            for t in range(TT):
                dve.wait_ge(vtr, t + 1)
                v.tensor_tensor(vb[:, t, :].rearrange("p (h c) -> p h c", h=H),
                                xbank[:, t * D:(t + 1) * D].rearrange("p (h c) -> p h c", h=H),
                                beta_half[:, t, :].unsqueeze(2).to_broadcast([P, H, P]), ALU.mult).then_inc(vb_ready, 1)
            slices_dve(2)
            dve.wait_ge(cum_exp, 1)
            for t in range(TT):
                dve.wait_ge(ktr, t + 1)
                v.tensor_tensor(kdec[:, t, :].rearrange("p (h c) -> p h c", h=H),
                                xbank[:, t * D:(t + 1) * D].rearrange("p (h c) -> p h c", h=H),
                                to_end[:, t, :].unsqueeze(2).to_broadcast([P, H, P]), ALU.mult).then_inc(kdec_ready, 1)
            slices_dve(2)
            for lev in range(1, 6):
                slices_dve(2)
                if lev < 5:
                    dve.wait_ge(lev_join, 2 * lev - 1)
                    v.tensor_tensor(inv[:], inv[:], uv(2), ALU.subtract).then_inc(inv_ready, 1)
                dve.wait_ge(lev_join, min(2 * lev, 9))
                v.tensor_tensor(invT[:], invT[:], uv(0), ALU.subtract).then_inc(inv_ready, 1)
                slices_dve(2)
            for n in range(NC):
                t, b = n // 2, n % 2
                rows = slice(b * C, (b + 1) * C)
                if n > 0:
                    dve.wait_ge(ks_done, 2 * n - 1)
                    v.tensor_tensor(R[rows, :], vb[rows, t, :], xbank[rows, 0:1024], ALU.subtract).then_inc(r_ready, 1)
                slices_dve(2)
                if n < NC - 1:
                    dve.wait_ge(ds_done, n + 1)
                    src = xbank[:, 0:1024].rearrange("p (h c) -> p h c", h=H)
                    if n == 0:
                        v.tensor_copy(S[:], src).then_inc(s_ready, 1)
                    else:
                        dve.wait_ge(s_scaled, n)
                        v.tensor_tensor(S[:], S[:], src, ALU.add).then_inc(s_ready, 1)
                slices_dve(1)
            for c in range(NC):
                kk = C if c == 0 else P
                scv = xbank[:, 0:1024].rearrange("p (c t) -> p c t", c=HP)[:, :, 0:kk]
                dve.wait_ge(sink_ready, 1)
                dve.wait_ge(sc_done, c + 1)
                if c:
                    dve.wait_ge(pt_done, c)
                    dve.wait_ge(sc_den, c)
                link(v.tensor_reduce(smax[:, 0, :], scv, AX_X, ALU.max))
                settle()
                link(v.tensor_tensor(smax[:, 1, :], smax[:, 0, :], sink[:], ALU.max))
                settle()
                link(v.tensor_tensor(sexp[:, 0, :], sink[:], smax[:, 1, :], ALU.subtract))
                settle()
                v.tensor_tensor(pr[:, :, 0:kk], scv, smax[:, 1, :].unsqueeze(2).to_broadcast([P, HP, kk]), ALU.subtract
                                ).then_inc(sc_shift, 1)
                slices_dve(1)
                dve.wait_ge(sc_exp, c + 1)
                link(v.tensor_reduce(sden[:, 0, :], pr[:, :, 0:kk], AX_X, ALU.add))
                settle()
                link(v.tensor_tensor(sden[:, 1, :], sden[:, 0, :], sexp[:, 0, :], ALU.add))
                settle()
                v.reciprocal(sden[:, 0, :], sden[:, 1, :]).then_inc(sc_den, 1)
                dve.wait_ge(sc_den, c + 1)
                v.tensor_tensor(pr[:, :, 0:kk], pr[:, :, 0:kk], sden[:, 0, :].unsqueeze(2).to_broadcast([P, HP, kk]),
                                ALU.mult).then_inc(pr_ready, 1)
                slices_dve(ATT_SLICES[c][0] + ATT_SLICES[c][1] - 1)
                if c == 0:
                    dve.wait_ge(o_squared, TT)
                    v.tensor_reduce(o_sum[:], o_sq[:].rearrange("p t (h c) -> p t h c", h=H), AX_X, ALU.add
                                    ).then_inc(o_summed, 1)
                dve.wait_ge(ya_hi, c + 1)
                hi, lo = pairs["ya"]
                v.tensor_tensor(lo[:, :, c * C:(c + 1) * C], xbank[:, 0:512].rearrange("p (c t) -> p c t", c=HP),
                                hi[:, :, c * C:(c + 1) * C].bitcast(F32), ALU.subtract).then_inc(ya_made, 1)
                slices_dve(ATT_SLICES[c][2])
                if c == 0:
                    slices_dve(2)
                    dve.wait_ge(o_rs_ready, 1)
                    for t in range(TT):
                        dve.wait_ge(o_gated, t + 1)
                        ov = o_tok[:, t, :].rearrange("p (h c) -> p h c", h=H)
                        v.tensor_tensor(ov, ov, o_rs[:, t, :].unsqueeze(2).to_broadcast([P, H, P]), ALU.mult
                                        ).then_inc(o_final, 1)
                    slices_dve(1)
                    pair_lo("yb", 1)
                    slices_dve(2)
            slices_dve(first_slice[last["wa"] + 1] + LEAD - at_slice[0])
            dve.wait_ge(p_hi, 1)
            v.tensor_tensor(pairs["p"][1][:], psX[:, 0, :].rearrange("p (k t) -> p k t", k=2),
                            pairs["p"][0][:].bitcast(F32), ALU.subtract).then_inc(p_made, 1)
            pair_lo("m", 2)
            slices_dve(first_slice[last["wo"] + 1] + LEAD - at_slice[0])

            def layer_norm(n, src, g_, b_, ready):
                for t in range(TT):
                    for q in range(2):
                        link(v.bn_stats(stats[:, t, q, :], src[:, t, q * W:(q + 1) * W]))
                settle()
                for t in range(TT):
                    ins = v.bn_aggr(mv[:, t, :], stats[:, t].rearrange("p q s -> p (q s)"))
                    if t == 0:
                        link(ins)
                settle()
                ins.then_inc(ln_var, 1)
                dve.wait_ge(ln_rstd, n + 1)
                for t in range(TT):
                    link(v.tensor_scalar(src[:, t, :], src[:, t, :], mv[:, t, 0:1], rstd[:, t:t + 1], ALU.subtract,
                                         ALU.mult))
                    settle()
                    link(v.tensor_tensor(src[:, t, :], src[:, t, :], g_[:], ALU.mult))
                    settle()
                    v.tensor_tensor(h_tok[:, t, :], src[:, t, :], b_[:], ALU.add).then_inc(h_ready, 1)

            dve.wait_ge(block_read, last["wo"] + 1)
            dve.wait_ge(ln1_loaded, 32)
            layer_norm(0, h_tok, ln1g, ln1b, h_ready)
            pair_lo("h", 3)
            slices_dve(8)
            dve.wait_ge(block_read, last["rt"] + 1)
            for t in range(TT):
                link(v.tensor_copy(g8[:, t, 0:N_GRP], lg[:, t, 0:N_GRP]))
            settle()
            for t in range(TT):
                link(v.max(top8[:, t, 0, :], g8[:, t, :]))
            settle()
            for t in range(TT):
                link(v.max_index(idx8[:, t, 0, :], top8[:, t, 0, :], g8[:, t, :]))
            settle()
            link(v.tensor_copy(idxf[:, :, 0, :], idx8[:, :, 0, :]))
            settle()
            for t in range(TT):
                link(v.tensor_scalar(g_hot[:, t, :], iota_e[:, 0:N_GRP], idxf[:, t, 0, 0:1], None, ALU.is_equal))
                link(v.tensor_scalar(g8[:, t, 0:N_GRP], g8[:, t, 0:N_GRP], top8[:, t, 0, 0:1], None, ALU.subtract))
            settle()
            link(v.tensor_scalar(g_hot[:], g_hot[:], -1.0, BIG, ALU.add, ALU.mult))
            settle()
            for t in range(TT):
                link(v.tensor_tensor(e_mask[:, t], lg[:, t, N_GRP:].rearrange("p (g e) -> p g e", g=N_GRP),
                                     g_hot[:, t, :].unsqueeze(2).to_broadcast([P, N_GRP, EPG]), ALU.add))
            settle()
            for t in range(TT):
                link(v.max(top8[:, t, 1, :], e_mask[:, t].rearrange("p g e -> p (g e)")))
            settle()
            for t in range(TT):
                link(v.max_index(idx8[:, t, 1, :], top8[:, t, 1, :], e_mask[:, t].rearrange("p g e -> p (g e)")))
            settle()
            link(v.tensor_copy(idxf[:, :, 1, :], idx8[:, :, 1, :]))
            v.tensor_tensor(r_small[:, 0, :], top8[:, :, 1, 1], top8[:, :, 1, 0], ALU.subtract).then_inc(rt_in, 1)
            settle()
            for t in range(TT):
                for k in range(2):
                    link(v.tensor_scalar(hot[:, k, t, :], iota_e[:], idxf[:, t, 1, k:k + 1], None, ALU.is_equal))
            settle()
            v.tensor_tensor(picked[:], hot[:, 0], hot[:, 1], ALU.add).then_inc(rt_picked, 1)
            dve.wait_ge(rt_exp, 1)
            link(v.tensor_reduce(r_small[:, 1, :], g8[:, :, 0:N_GRP], AX_X, ALU.add))
            link(v.tensor_scalar(r_small[:, 2, :], r_small[:, 0, :], 1.0, None, ALU.add))
            settle()
            link(v.tensor_tensor(r_small[:, 3, :], r_small[:, 1, :], r_small[:, 2, :], ALU.mult))
            settle()
            link(v.reciprocal(r_small[:, 4, :], r_small[:, 3, :]))
            settle()
            link(v.tensor_tensor(r_small[:, 5, :], r_small[:, 4, :], r_small[:, 0, :], ALU.mult))
            settle()
            for t in range(TT):
                link(v.tensor_scalar(hot[:, 1, t, :], hot[:, 1, t, :], r_small[:, 5, t:t + 1], None, ALU.mult))
            settle()
            for t in range(TT):
                link(v.scalar_tensor_tensor(comb[:, t, 0:N_EXP], hot[:, 0, t, :], r_small[:, 4, t:t + 1],
                                            hot[:, 1, t, :], ALU.mult, ALU.add))
            slices_dve(4)
            dve.wait_ge(rt_cum, 1)
            pos = xbank[:, 0:2 * N_EXP].rearrange("p (t e) -> p t e", t=TT)
            dve.wait_ge(rt_picked, 1)
            link(v.scalar_tensor_tensor(posm[:, :, 0:N_EXP], pos, 1.0, picked[:], ALU.add, ALU.mult))
            link(v.tensor_reduce(n_max[:], xbank[:, 2 * N_EXP:3 * N_EXP], AX_X, ALU.max))
            settle()
            link(v.tensor_scalar(posm[:, :, 0:N_EXP], posm[:, :, 0:N_EXP], -1.0, None, ALU.add))
            settle()
            v.tensor_scalar(more[:], n_max[:], float(SLOTS), None, ALU.is_gt).then_inc(rt_done, 1)
            slices_dve(len(slices) + LEAD + 5 - at_slice[0])
            for t in range(TT):
                dve.wait_ge(hk_hi_ready, t + 1)
                v.tensor_tensor(hk_lo[:, t, :], h_tok[:, t, :], hk_hi[:, t, :].bitcast(F32), ALU.subtract
                                ).then_inc(hk_ready, 1)
            dve.wait_ge(block_read, len(blocks))
            dve.wait_ge(acc_scaled, 1)
            v.scalar_tensor_tensor(acc[:], th_p[:], 0.5, acc[:], ALU.mult, ALU.add).then_inc(acc_added, 1)

            def select(g, e):
                v.tensor_tensor(sel[:].rearrange("p t (a s) -> p t a s", a=2),
                                iota_s[:].unsqueeze(1).unsqueeze(1).to_broadcast([P, TT, 2, SLOTS]),
                                posm[:, :, e].unsqueeze(3).to_broadcast([P, TT, 2, SLOTS]), ALU.is_equal
                                ).then_inc(sel_ready, 1)

            def expert_pass(r):
                if not isinstance(r, int):
                    dve.wait_ge(selt_done, 17 * r)
                    dve.wait_ge(sel_ready, 17 * r)
                    v.tensor_scalar(posm[:], posm[:], -float(SLOTS), None, ALU.add).then_inc(pass_shift, 1)
                    dve.wait_ge(pass_shift, r)
                select(17 * r, slice(0, 2))

                def add_outputs(m, hf):
                    cs = slice(hf * W, (hf + 1) * W)
                    for t in range(TT):
                        dve.wait_ge(sc_out, 4 * m + 2 * hf + t + 1)
                        dve.wait_ge(acc_added, 4 * m + 1)
                        v.tensor_tensor(acc[:, t, cs], acc[:, t, cs], psX[:, t, :], ALU.add).then_inc(acc_added, 1)

                def expert_pair(i, par, first=False):
                    n = 16 * r + 2 * i + par
                    g = 17 * r + 2 * i + par
                    dve.wait_ge(selt_done, g + 1)
                    select(g + 1, bass.ds(4 * i + 2 * par + 2, 2))
                    for a in range(2):
                        dve.wait_ge(gu_done, 2 * n + a + 1)
                        v.tensor_copy(gus[:, a, :], psD[:, 2 + a, :]).then_inc(gus_ready, 1)
                        if not first:
                            add_outputs(n - 1, a)
                    for a in range(2):
                        dve.wait_ge(silu_done, 2 * n + a + 1)
                        v.tensor_tensor(he[:, a], psX[:, a, 2 * C:4 * C].rearrange("p (k s) -> p k s", k=2),
                                        sg[:, a], ALU.mult).then_inc(he_ready, 1)
                    for hf in range(2):
                        dve.wait_ge(yhi_ready, 2 * n + hf + 1)
                        cs = slice(hf * W, (hf + 1) * W)
                        v.scalar_tensor_tensor(y_lo[:, cs], psX[:, 2 + hf, :], w_slot[:, par:par + 1],
                                               y_hi[:, cs].bitcast(F32), ALU.mult, ALU.subtract
                                               ).then_inc(ylo_ready, 1)

                expert_pair(0, 0, first=True)
                expert_pair(0, 1)
                with dve.Fori(1, N_EXP // 4) as i:
                    for par in range(2):
                        expert_pair(i, par)
                for hf in range(2):
                    add_outputs(16 * r + 15, hf)

            expert_pass(0)
            dve.wait_ge(rt_done, 1)
            again = dve.value_load(more[0:1, 0:1])
            with dve.If(again > 0):
                with dve.Fori(1, PASSES) as r:
                    expert_pass(r)
                dve.wait_ge(acc_added, 64 * PASSES + 1)
            dve.wait_ge(acc_added, 65)
            dve.wait_ge(ln2_loaded, 32)
            layer_norm(1, acc, ln2g, ln2b, h_ready)

        @block.gpsimd
        def _(pool):
            g_ = nc.gpsimd
            count_up, settle = chain(pool, pool_s)

            def link(ins):
                count_up(ins)
                settle()

            def keep(t_, pattern, base, cm, fill=0.0, op=ALU.is_ge):
                link(g_.affine_select(out=t_, in_=t_, pattern=pattern, compare_op=op, fill=fill, base=base,
                                      channel_multiplier=cm))

            link(g_.memset(ident[:], 0.0))
            keep(ident[:], [[-1, P]], 0, 1, 1.0, ALU.not_equal)
            pool.nop().then_inc(ident_ready, 1)
            link(g_.memset(conv_in[:, :, :, 0:TAPS - 1], 0.0))
            link(g_.memset(eps_l2[:], 4 * NORM_EPS))
            link(g_.memset(eps_ln[:], LN_EPS))
            link(g_.memset(eps_norm[:], NORM_EPS))
            link(g_.memset(one[:], 1.0))
            pool.nop().then_inc(biases_ready, 1)
            for m in (ones, half_rows):
                link(g_.memset(m[:], 1.0))
            link(g_.memset(stack_eye[:], 0.0))
            link(g_.memset(tri[:], 1.0))
            link(g_.memset(before[:], 1.0))
            link(g_.memset(chunk1[:], 1.0))
            link(g_.memset(level_mask[:], 1.0))
            link(g_.memset(mask_upper[:], 0.0))
            link(g_.memset(mask_sub[:], -BIG))
            link(g_.memset(g8[:], -BIG))
            link(g_.memset(comb[:], 0.0))
            link(g_.memset(posm[:], -1.0))
            settle()

            keep(tri[:], [[1, P]], 0, -1)
            keep(before[:], [[1, P]], -1, -1)
            keep(half_rows[:, 0, :], [[0, P]], C - 1, -1)
            keep(half_rows[:, 1, :], [[0, P]], -C, 1)
            for b in range(2):
                keep(stack_eye[:], [[-1, C]], -b * C, 1, 1.0, ALU.not_equal)
                settle()
            settle()
            keep(tri[:, C:P], [[0, C]], -C, 1)
            keep(chunk1[:, C:P], [[0, C]], -C, 1)
            settle()
            keep(chunk1[:, 0:C], [[0, C]], C - 1, -1)
            for b in range(2):
                rows = slice(b * C, (b + 1) * C)
                keep(mask_upper[rows, :], [[1, C]], 0, -1, -BIG)
                keep(mask_sub[rows, :].rearrange("p (a two) -> p two a", two=2)[:, 0], [[-2, C // 2]], -1, 1, 0.0,
                     ALU.not_equal)
                for lev in range(6):
                    s_ = 1 << lev
                    m = level_mask[rows, lev, :].rearrange("p (a two s) -> p a two s", two=2, s=s_)
                    link(g_.memset(m[:, :, 0, :], 0.0))
                    for lo_, base, cm in ((True, 0, 1), (False, s_ - 1, -1)):
                        settle()
                        step = -2 * s_ if lo_ else 2 * s_
                        keep(m[:, :, 1, :], [[step, C // (2 * s_)], [0, s_]], base, cm)
            link(g_.iota(iota_e[:], [[1, N_EXP]], base=0, channel_multiplier=0, allow_small_or_imprecise_dtypes=True))
            link(g_.iota(iota_s[:], [[1, SLOTS]], base=0, channel_multiplier=0, allow_small_or_imprecise_dtypes=True))
            settle()
            pool.nop().then_inc(consts, 1)
            pool.wait_ge(small_loaded, 16 * 5)
            g_.tensor_scalar(norm_g[:], norm_g[:], 0.5, None, ALU.mult).then_inc(z_free, 1)
            for n in range(4):
                pool.wait_ge(conv_out, n + 1)
                if n:
                    pool.wait_ge(sq_summed, n)
                src = (kT if n < 2 else qT)[:, 4 * (n % 2):4 * (n % 2) + 4, :]
                g_.tensor_tensor(sq[:], src, src, ALU.mult).then_inc(squared, 1)
            pool.wait_ge(dec_raw, 1)
            d4 = lambda m: m.unsqueeze(1).to_broadcast([P, U, C])
            g_.tensor_tensor(dec_up[:], d4(mask_upper[:]), dec_sub[:], ALU.subtract).then_inc(dec_masked, 1)
            g_.tensor_tensor(dec_sub[:], dec_sub[:], d4(mask_sub[:]), ALU.add).then_inc(dec_masked, 1)
            pool.wait_ge(gram, 3)
            pool.wait_ge(eg_ready, 1)
            for m in (kbT, qT):
                g_.tensor_tensor(m[:], m[:], eg[:], ALU.mult).then_inc(eg_used, 1)
            pool.wait_ge(gram_read, 3)
            for lev in range(1, 6):
                if lev > 2:
                    pool.wait_ge(lev_prod, lev - 2)
                g_.tensor_tensor(LT_lev[:, lev % 2], LT[:], d4(level_mask[:, lev, :]), ALU.mult).then_inc(lev_masked, 1)
            for n in range(1, NC - 1):
                pool.wait_ge(ks_done, 2 * n)
                g_.tensor_tensor(S[:], S[:], g_chunk[:, n, :].unsqueeze(2).to_broadcast([P, H, P]), ALU.mult
                                 ).then_inc(s_scaled, 1)
            for n in range(2):
                pool.wait_ge(block_read, names.index("z") + n + 1)
                zv = zg[:, :, n * W:(n + 1) * W].rearrange("p t (h c) -> p t h c", c=P)
                for t in range(TT):
                    ins = g_.tensor_tensor(zv[:, t], zv[:, t], norm_g[:].unsqueeze(1).to_broadcast([P, W // P, P]),
                                           ALU.mult)
                ins.then_inc(z_norm, 1)
            for t in range(TT):
                pool.wait_ge(o_read, 2 * t + 2)
                if t == 0:
                    pool.wait_ge(ks_done, 2 * (NC - 1))
                g_.tensor_tensor(o_sq[:, t, :], o_tok[:, t, :], o_tok[:, t, :], ALU.mult).then_inc(o_squared, 1)
            pool.wait_ge(z_norm, 2)
            for t in range(TT):
                pool.wait_ge(o_squared, t + 1)
                g_.tensor_tensor(o_tok[:, t, :], o_tok[:, t, :], zg[:, t, :], ALU.mult).then_inc(o_gated, 1)
            pool.wait_ge(x2_loaded, 16)
            g_.tensor_scalar(x_again[:], x_again[:], ALPHA, None, ALU.mult).then_inc(ax_ready, 1)
            for n in range(2):
                pool.wait_ge(block_read, names.index("wa") + n + 1)
                cs = slice(n * W, (n + 1) * W)
                g_.tensor_tensor(merged[:, :, cs], merged[:, :, cs], gated_a[:], ALU.add).then_inc(merged_ready, 1)
            pool.wait_ge(h_ready, TT)
            g_.tensor_scalar(acc[:], h_tok[:], ALPHA, None, ALU.mult).then_inc(acc_scaled, 1)


_INS = ["x", "p", "w_in", "attn_sink", "conv_w", "a_log", "dt_bias", "gdn_norm_g", "w_branch_a", "w_branch_b",
        "w_out", "ln1_g", "ln1_b", "w_route_group", "b_route_group", "w_route_expert", "b_route_expert",
        "w_exp_gate", "w_exp_up", "w_exp_down", "w_ple_gate", "b_ple_gate", "w_ple_proj", "ln2_g", "ln2_b"]
_OUTS = [((1, 256, 1024), "float32")]


def kernel(**inputs):
    import numpy as _np
    import concourse.bacc as _bacc
    from concourse import mybir as _mybir
    from concourse.bass_utils import run_bass_kernel_spmd as _run

    nc = _bacc.Bacc("TRN2", target_bir_lowering=False, num_devices=1)
    arrays, args = {}, []
    for name in _INS:
        a = _np.ascontiguousarray(inputs[name])
        arrays[f"in_{name}_dram"] = a
        args.append(nc.dram_tensor(f"in_{name}_dram", a.shape, _mybir.dt.from_np(a.dtype), kind="ExternalInput").ap())
    for i, (shape, dtype) in enumerate(_OUTS):
        dt = _mybir.dt.from_np(_np.dtype(dtype))
        args.append(nc.dram_tensor(f"out_{i}_dram", shape, dt, kind="ExternalOutput").ap())
    build(nc, *args)
    r = _run(nc, [arrays], core_ids=[0])
    return r.results[0]["out_0_dram"]
```

```python
import math
from contextlib import ExitStack

import concourse.bass as bass
from concourse import mybir
from concourse.alu_op_type import AluOpType as ALU

F32 = mybir.dt.float32
F32R = mybir.dt.float32r
I32 = mybir.dt.int32
U32 = mybir.dt.uint32
ACT = mybir.ActivationFunctionType
AX_X = mybir.AxisListType.X

P = 128
KB = 1024
D = 1024
T = 256
TT = T // P
KT = D // P
C = 64
NC = T // C
HALVES = (slice(0, 4), slice(4, 8))
SCAN_SLICES = ((1, 1, 1), (1, 1, 1), (1, 1, 1), (1, 2, 0))
ATT_SLICES = ((4, 2, 1), (5, 2, 2), (5, 2, 2), (5, 2, 2))
TURN_SLICES = 1
H = 8
HP = 8
KVH = 4
TAPS = 4
U = H * TT
N_EXP = 32
N_GRP = 4
EPG = N_EXP // N_GRP
F = 256
SLOTS = 64
PASSES = T // SLOTS
PLE = 256
ALPHA = 2.0 ** 0.25
LN_EPS = 1e-5
NORM_EPS = 1e-6
BIG = 1e30
W = 512
NARROW = {"ab": 1, "rt": 2}

QA, KA, VA, QB, KB_, VB, ZB, BETA, GA, GB = 0, 1024, 1280, 1536, 2560, 3584, 4608, 5632, 5648, 6672

LEAD = 5
RING = 8
CHUNK = 4
RAWS = 4


def plan_blocks():
    b = [("ab", "x", KT, BETA, 16)]
    b += [("k", "x", KT, KB_ + W * i, W) for i in range(2)]
    b += [("q", "x", KT, QB + W * i, W) for i in range(2)]
    b += [("v", "x", KT, VB + W * i, W) for i in range(2)]
    b += [("qa", "x", KT, QA + W * i, W) for i in range(2)]
    b += [("kva", "x", KT, KA, W)]
    b += [("z", "x", KT, ZB + W * i, W) for i in range(2)]
    b += [("ga", "x", KT, GA + W * i, W) for i in range(2)]
    b += [("gb", "x", KT, GB + W * i, W) for i in range(2)]
    b += [("wb", "yb", KT, W * i, W) for i in range(2)]
    b += [("wa", "ya", KT, W * i, W) for i in range(2)]
    b += [("wo", "m", KT, W * i, W) for i in range(2)]
    b += [("pp", "p", 2, W * i, W) for i in range(2)]
    b += [("rt", "h", KT, 0, N_GRP + N_EXP)]
    b += [("pg", "h", KT, W * i, W) for i in range(2)]
    return b


def build(nc, x, p, w_in, attn_sink, conv_w, a_log, dt_bias, gdn_norm_g, w_branch_a, w_branch_b, w_out,
          ln1_g, ln1_b, w_route_group, b_route_group, w_route_expert, b_route_expert,
          w_exp_gate, w_exp_up, w_exp_down, w_ple_gate, b_ple_gate, w_ple_proj, ln2_g, ln2_b, out):
    blocks = plan_blocks()
    names = [b[0] for b in blocks]
    slices = []
    for b, blk in enumerate(blocks):
        if blk[0] in NARROW:
            per = NARROW[blk[0]]
            for kt in range(KT):
                slices += [(b, kt)] + ([(b + 1, kt // per)] if (kt + 1) % per == 0 else [])
        else:
            slices += [(b, kt) for kt in range(blk[2]) if (b, kt) not in slices]
    first_slice = [slices.index((b, 0)) for b in range(len(blocks))]
    end_slice = {slices.index((b, blk[2] - 1)): b for b, blk in enumerate(blocks)}
    loads, place = [], {}
    for b, kt in slices:
        most = KT if blocks[b][0] in NARROW else CHUNK
        if kt % most == 0:
            loads.append((b, kt, min(most, blocks[b][2] - kt)))
    for m, (b, k0, n) in enumerate(loads):
        for k in range(n):
            place[slices.index((b, k0 + k))] = (m, k)
    last_load = [max(m for m, l in enumerate(loads) if l[0] == b) for b in range(len(blocks))]
    raw_place = [m % RAWS for m in range(len(loads))]
    raw_place[-5:] = [0, 1, 2, 3, 2]
    load_before = [max([q for q in range(m) if raw_place[q] == raw_place[m]], default=None) for m in range(len(loads))]
    last_slice_of = [max(j for j in place if place[j][0] == m) for m in range(len(loads))]

    ctx = ExitStack()
    with ctx:
        BASE = 17 * KB
        cursor = [BASE]

        def at(name, shape, dt, off):
            return nc.alloc_sbuf_tensor_at(name, shape, dt, offset=off)

        def perm(name, shape, dt=F32):
            n = 4
            for s in shape[1:]:
                n *= s
            off = cursor[0]
            cursor[0] += (n + 31) // 32 * 32
            return at(name, shape, dt, off)

        ident = perm("ident", [P, P])
        before = perm("before", [P, P])
        ones = perm("ones", [P, P])
        stack_eye = perm("stack_eye", [P, C])
        conv_c = perm("conv_c", [P, TAPS, 24])
        sink = perm("sink", [P, HP])
        sink_all = perm("sink_all", [P, 2 * HP])
        alog = perm("alog", [P, H])
        dtb = perm("dtb", [P, H])
        norm_g = perm("norm_g", [P, P])
        ab = perm("ab", [P, TT, 16])
        beta = perm("beta", [P, TT, H])
        beta_half = perm("beta_half", [P, TT, H])
        soft = perm("soft", [P, TT, H])
        softb = perm("softb", [P, TT, H])
        decay_g = perm("decay_g", [P, TT, H])
        neg_a = perm("neg_a", [P, H])
        gc = perm("gc", [P, TT, H])
        to_end = perm("to_end", [P, TT, H])
        g_chunk = perm("g_chunk", [P, NC, H])
        smax = perm("smax", [P, 2, HP])
        sden = perm("sden", [P, 2, HP])
        sexp = perm("sexp", [P, 2, HP])
        o_sum = perm("o_sum", [P, TT, H])
        o_rs = perm("o_rs", [P, TT, H])
        stats = perm("stats", [P, TT, 2, 6])
        mv = perm("mv", [P, TT, 2])
        rstd = perm("rstd", [P, TT])
        eps_l2 = perm("eps_l2", [P, 2])
        eps_ln = perm("eps_ln", [P, 1])
        eps_norm = perm("eps_norm", [P, 1])
        one = perm("one", [P, 1])
        rt_b = perm("rt_b", [P, N_GRP + N_EXP])
        iota_e = perm("iota_e", [P, N_EXP])
        iota_s = perm("iota_s", [P, SLOTS])
        lg = perm("lg", [P, TT, N_GRP + N_EXP])
        g8 = perm("g8", [P, TT, 8])
        top8 = perm("top8", [P, TT, 2, 8])
        idx8 = perm("idx8", [P, TT, 2, 8], U32)
        idxf = perm("idxf", [P, TT, 2, 8])
        g_hot = perm("g_hot", [P, TT, N_GRP])
        e_mask = perm("e_mask", [P, TT, N_GRP, EPG])
        hot = perm("hot", [P, 2, TT, N_EXP])
        r_small = perm("r_small", [P, 8, TT])
        picked = perm("picked", [P, TT, N_EXP])
        comb = perm("comb", [P, TT, N_EXP + 2])
        posm = perm("posm", [P, TT, N_EXP + 4])
        n_tok = perm("n_tok", [P, N_EXP])
        n_max = perm("n_max", [P, 1])
        more = perm("more", [P, 1], I32)
        w_slot = perm("w_slot", [P, 2])
        STREAM = (cursor[0] + 127) // 128 * 128
        raw = at("raw", [P, RAWS, CHUNK, W], F32, STREAM)
        w_hi = at("w_hi", [P, RING, W], F32R, STREAM + 32 * KB)
        w_lo = at("w_lo", [P, RING, W], F32R, STREAM + 48 * KB)
        XT = STREAM + 64 * KB
        A0 = XT + 16 * KB

        def area(name, shape, kb, dt=F32):
            return at(name, shape, dt, A0 + int(kb * KB))

        def pair(name, off, kt=KT):
            return (at(name + "_hi", [P, kt, T], F32R, off), at(name + "_lo", [P, kt, T], F32R, off + kt * KB))

        pairs = {"x": pair("xT", XT), "ya": pair("yaT", A0 + 76 * KB), "yb": pair("ybT", A0),
                 "m": pair("mT", XT), "h": pair("hT", A0 + 76 * KB), "p": pair("pT", A0 + 110 * KB, 2)}
        tri = area("tri", [P, P], 108)
        chunk1 = area("chunk1", [P, P], 108.5)
        half_rows = area("half_rows", [P, 2, P], 109)
        level_mask = area("level_mask", [P, 6, C], 110)
        mask_upper = area("mask_upper", [P, C], 111.5)
        mask_sub = area("mask_sub", [P, C], 111.75)
        conv_rows = area("conv_rows", [P, P], 112)
        x_tok = area("x_tok", [P, TT, D], 92)
        kbT = area("kbT", [P, H, T], 0)
        qT = area("qT", [P, H, T], 8)
        vb = area("vb", [P, TT, D], 16)
        kdec = area("kdec", [P, TT, D], 24)
        invT = area("invT", [P, U, C], 32)
        attT = area("attT", [P, U, C], 36)
        S = area("S", [P, H, P], 40)
        R = area("R", [P, D], 44)
        v_new = area("v_new", [P, D], 48)
        o_tok = area("o_tok", [P, TT, D], 52)
        zg = area("zg", [P, TT, D], 60)
        th_a = area("th_a", [P, TT, D], 68)
        conv_in = area("conv_in", [P, 2, 4, TAPS - 1 + T], 60)
        conv_y = area("conv_y", [P, 4, T], 44)
        conv_t = area("conv_t", [P, 4, T], 48)
        sq = area("sq", [P, 4, T], 40)
        rs = area("rs", [P, 2, 4, T], 52)
        kT = area("kT", [P, H, T], 76)
        vT = area("vT", [P, H, T], 84)
        eg = area("eg", [P, H, T], 68)
        dec_sub = area("dec_sub", [P, U, C], 52)
        dec_up = area("dec_up", [P, U, C], 56)
        LT = area("LT", [P, U, C], 40)
        prod = area("prod", [P, U, C], 44)
        inv = area("inv", [P, U, C], 48)
        LT_lev = area("LT_lev", [P, 2, U, C], 52)
        qaT = area("qaT", [P, HP, T], 92)
        kaT = area("kaT", [P, KVH, T], 100)
        va = area("va", [P, 3, 256], 104)
        pr = area("pr", [P, HP, P], 107)
        prT = area("prT", [P, HP, P], 111)
        th_b = area("th_b", [P, TT, D], 40)
        merged = area("merged", [P, TT, D], 16)
        gated_a = area("gated_a", [P, TT, W], 92)
        x_again = area("x_again", [P, TT, D], 24)
        h_tok = area("h_tok", [P, TT, D], 32)
        ln1g = area("ln1g", [P, D], 100)
        ln1b = area("ln1b", [P, D], 104)
        p_tok = area("p_tok", [P, TT, PLE], 108)
        pleb = area("pleb", [P, D], 72)
        ln2g = area("ln2g", [P, D], 108)
        ln2b = area("ln2b", [P, D], 112)
        gu_off = [A0, A0 + 56 * KB, STREAM, STREAM + 16 * KB]
        dn_off = [A0 + 16 * KB, A0 + 92 * KB, A0 + 100 * KB, A0 + 24 * KB]
        w_gu = [at(f"w_gu{s}", [P, KT, 2, F], F32, gu_off[s]) for s in range(4)]
        w_dn = [at(f"w_dn{s}", [P, 2, D], F32, dn_off[s]) for s in range(4)]
        acc = at("acc", [P, TT, D], F32, XT)
        th_p = at("th_p", [P, TT, D], F32, XT + 8 * KB)
        hk_hi = area("hk_hi", [P, TT, D], 40, F32R)
        hk_lo = area("hk_lo", [P, TT, D], 48, F32R)
        M0 = STREAM + 48 * KB
        gath = area("gath", [P, 2, KT, 2 * P], 76)
        y_hi = at("y_hi", [P, D], F32R, M0 + 4 * KB)
        y_lo = at("y_lo", [P, D], F32R, M0 + 8 * KB)
        gus = at("gus", [P, 2, W], F32, M0 + 12 * KB)
        sg = at("sg", [P, 2, 2, SLOTS], F32, M0)
        he = at("he", [P, 2, 2, SLOTS], F32, M0 + 1 * KB)
        selT = at("selT", [P, 2, TT, P], F32R, M0 + 2 * KB)
        sel_quad = area("sel_quad", [P, TT, 2 * P], 116, F32R)
        sel = area("sel", [P, TT, P], 118, F32R)

        psD = ctx.enter_context(nc.psum_tensor("psD", [P, 4, 512], F32))
        psX = ctx.enter_context(nc.psum_tensor("psX", [P, 4, 512], F32))
        xbank = psX[:].rearrange("p b n -> p (b n)")
        dbank = psD[:].rearrange("p b n -> p (b n)")

        def block_bank(b):
            o = (len(blocks) - b) % 2 * 1024
            return dbank[:, o:o + 1024]

        def sem(name):
            return ctx.enter_context(nc.semaphore(name))

        load_sem = [sem(f"raw_loaded{m}") for m in range(RAWS)]
        hi_ready, lo_ready, slice_used = sem("hi_ready"), sem("lo_ready"), sem("slice_used")
        block_done, block_read = sem("block_done"), sem("block_read")
        x_loaded = [sem(f"x_loaded{hf}") for hf in range(2)]
        small_loaded, bias_loaded = sem("small_loaded"), sem("bias_loaded")
        ident_ready, biases_ready, consts = sem("ident_ready"), sem("biases_ready"), sem("consts")
        tr_done, hi_made, lo_made = sem("transposed"), sem("pair_hi_made"), sem("pair_lo_made")
        vec, act_s, pool_s = sem("vector_chain"), sem("scalar_chain"), sem("pool_chain")

        def wait(eng, s, v):
            if not isinstance(v, int) or v > 0:
                eng.wait_ge(s, v)

        def chain(eng, s):
            n = [0]

            def link(ins):
                n[0] += 1
                ins.then_inc(s, 1)
                return ins

            def settle():
                if n[0]:
                    eng.wait_ge(s, n[0])
            return link, settle

        kv_b = names.index("kva")
        last = {n: len(names) - 1 - names[::-1].index(n) for n in set(names)}
        wa_mid = first_slice[last["wa"]] + 3
        wo_mid = first_slice[last["wo"] - 1] + 3
        pp_mid = first_slice[last["pp"]] + 1
        lo_before = {"x": 0, "yb": 4, "m": 8, "h": 12}
        reader = {n: "vector" if n in ("ab", "z", "wb", "wa", "wo", "rt", "pg") else "scalar" for n in names}

        def readers_in_order(eng, b):
            if b and reader[names[b - 1]] != reader[names[b]]:
                eng.wait_ge(block_read, b)

        conv_ready, conv_th, conv_out = sem("conv_ready"), sem("conv_tanh"), sem("conv_out")
        squared, sq_summed, rs_ready, normed = sem("squared"), sem("sq_summed"), sem("rs_ready"), sem("normed")
        cw_tr, cw_ready = sem("conv_taps_turned"), sem("conv_taps_ready")
        ab1, ab2, ab3, ab4, beta_ready = (sem("soft_in"), sem("soft_exp"), sem("decay_ready"), sem("beta_exp"),
                                          sem("beta_ready"))
        cum_done, cum_read, cum_exp = sem("cum_done"), sem("cum_read"), sem("cum_exp")
        brow, kb_ready = sem("beta_rows"), sem("kb_ready")
        grow, eg_ready, dec_raw, dec_masked, dec_ready = (sem("gc_rows"), sem("eg_ready"), sem("dec_raw"),
                                                          sem("dec_masked"), sem("dec_ready"))
        gram, gram_read, eg_used = sem("grams"), sem("grams_read"), sem("eg_applied")
        vtr, vb_ready, ktr, kdec_ready = sem("v_turned"), sem("vb_ready"), sem("k_turned"), sem("kdec_ready")
        lev_masked, lev_prod, lev_copied, lev_join, inv_ready = (
            sem("level_masked"), sem("level_product"), sem("level_copied"), sem("level_joined"), sem("inverse_level"))
        ks_done, r_ready, vn_done, vn_ready, o_done, o_read, ds_done, s_scaled, s_ready = (
            sem("ks_done"), sem("r_ready"), sem("vn_done"), sem("vn_ready"), sem("o_done"), sem("o_read"),
            sem("ds_done"), sem("s_scaled"), sem("s_ready"))
        o_squared, o_summed, o_rs_ready, o_final = sem("o_squared"), sem("o_summed"), sem("o_rs"), sem("o_final")
        o_gated, o_squared_act = sem("o_gated"), sem("o_squared_act")
        sc_done, sc_shift, sc_exp, sc_den, pr_ready, pt_done, pt_read, pv_done, ya_hi, ya_made = (
            sem("scores_done"), sem("scores_shifted"), sem("scores_exp"), sem("scores_den"), sem("probs_ready"),
            sem("probs_turned"), sem("probs_turned_read"), sem("pv_done"), sem("ya_hi"), sem("ya_made"))
        z_th, z_norm, ax_ready, x2_loaded, ln1_loaded = (sem("z_tanh"), sem("z_norm"), sem("ax_ready"),
                                                         sem("x_again_loaded"), sem("ln1_loaded"))
        gb_ready, merged_ready = sem("gated_a_ready"), sem("merged_ready")
        ln_var, ln_rstd, ln_centred, h_ready = sem("ln_var"), sem("ln_rstd"), sem("ln_centred"), sem("h_ready")
        p_loaded, p_turned, p_hi, p_made = sem("p_loaded"), sem("p_turned"), sem("p_hi"), sem("p_made")
        pleb_loaded, ln2_loaded, pg_in, pg_th = sem("pleb_loaded"), sem("ln2_loaded"), sem("ple_in"), sem("ple_tanh")
        ple_added, hk_hi_ready, hk_ready = sem("ple_added"), sem("hk_hi_ready"), sem("hk_ready")
        rt_in, rt_exp, rt_picked, rt_cum, rt_done = (sem("route_logits"), sem("route_exp"), sem("route_picked"),
                                                     sem("route_cum"), sem("route_done"))
        gu_load = [sem(f"w_gu_loaded{s_}") for s_ in range(4)]
        dn_load = [sem(f"w_dn_loaded{s_}") for s_ in range(4)]
        stats_made = sem("stats_made")
        quad_ready = sem("quad_selection_ready")
        sel_ready, gather_done, gath_ready, gu_done, gus_ready, t_done, silu_done, he_ready = (
            sem("sel_ready"), sem("gather_done"), sem("gathered_ready"), sem("gate_up_done"), sem("gate_up_read"),
            sem("turned_done"), sem("silu_done"), sem("hidden_ready"))
        dn_done, yhi_ready, ylo_ready, selt_done, selt_ready, sc_out, acc_added = (
            sem("down_done"), sem("y_hi_ready"), sem("y_lo_ready"), sem("sel_turned"), sem("sel_turned_read"),
            sem("scattered"), sem("acc_added"))
        stored, sink_ready, z_free, pass_shift = sem("stored"), sem("sink_ready"), sem("norm_gain_halved"), sem("pass_shift")
        o_sq = area("o_sq", [P, TT, D], 40)
        load_counts, totals = [], [0] * RAWS
        for m, (b_, _, _) in enumerate(loads):
            totals[raw_place[m]] += 32 if names[b_] == "rt" else 16
            load_counts.append(totals[raw_place[m]])

        def load_count(m):
            return load_counts[m]

        def dtb_rows():
            return dtb[:].unsqueeze(1).to_broadcast([P, TT, H])

        def neg_rows():
            return neg_a[:].unsqueeze(1).to_broadcast([P, TT, H])

        def win_slices(b, k0, n):
            name, _, _, off, wd = blocks[b]
            src = {"wa": w_branch_a, "wb": w_branch_b, "wo": w_out, "pg": w_ple_gate, "pp": w_ple_proj}.get(name, w_in)
            return src[0].rearrange("(k p) n -> p k n", p=P)[:, k0:k0 + n, off:off + wd]

        def raw_slice(j):
            m, q = place[j]
            wd = blocks[slices[j][0]][4]
            if blocks[slices[j][0]][0] in NARROW:
                return raw[:, raw_place[m]].rearrange("p k n -> p (k n)")[:, q * wd:(q + 1) * wd]
            return raw[:, raw_place[m], q, 0:wd]

        def split_slice(j):
            b = slices[j][0]
            wd = blocks[b][4]
            if blocks[b][0] in NARROW:
                return w_hi[:, j % RING, 0:wd], w_hi[:, j % RING, wd:2 * wd]
            return w_hi[:, j % RING, 0:wd], w_lo[:, j % RING, 0:wd]

        def bc(ap, dims):
            return ap.to_broadcast(dims)

        block = ctx.enter_context(nc.Block())

        @block.sync
        def _(sp):
            for hf in range(2):
                cs = slice(hf * W, (hf + 1) * W)
                sp.dma_start(x_tok[:, :, cs], x[0].rearrange("(t p) d -> p t d", p=P)[:, :, cs]
                             ).then_inc(x_loaded[hf], 16)

            def load(m):
                b, k0, n = loads[m]
                wd = blocks[b][4]
                if load_before[m] is not None:
                    sp.wait_ge(lo_ready, last_slice_of[load_before[m]] + 1)
                dst = raw[:, raw_place[m], 0:n, 0:wd] if names[b] not in NARROW else (
                    raw[:, raw_place[m]].rearrange("p k n -> p (k n)")[:, 0:n * wd].rearrange("p (k n) -> p k n", n=wd))
                if names[b] == "rt":
                    rg = w_route_group[0].rearrange("(k p) n -> p k n", p=P)
                    re = w_route_expert[0].rearrange("(k p) n -> p k n", p=P)
                    sp.dma_start(dst[:, :, 0:N_GRP], rg).then_inc(load_sem[raw_place[m]], 16)
                    sp.dma_start(dst[:, :, N_GRP:], re).then_inc(load_sem[raw_place[m]], 16)
                else:
                    sp.dma_start(dst, win_slices(b, k0, n)).then_inc(load_sem[raw_place[m]], 16)

            def load_gu(s_, e):
                for j, src in enumerate((w_exp_gate, w_exp_up)):
                    sp.dma_start(w_gu[s_][:, :, j, :],
                                 src[0, e].rearrange("o (k p) n -> p (o k) n", p=P)).then_inc(gu_load[s_], 16)

            def load_dn(s_, e):
                sp.dma_start(w_dn[s_][:], w_exp_down[0, e].rearrange("o (k p) n -> p (o k) n", p=P)
                             ).then_inc(dn_load[s_], 16)

            for m, (b, k0, n) in enumerate(loads):
                load(m)
                if m != last_load[b]:
                    continue
                if b == last["wb"]:
                    sp.wait_ge(ds_done, NC - 1)
                    sp.dma_start(x_again[:], x[0].rearrange("(t q) d -> q t d", q=P)).then_inc(x2_loaded, 16)
                if b == last["wa"]:
                    sp.wait_ge(ya_made, NC)
                    sp.dma_start(ln1g[:], ln1_g[0:1].to_broadcast([P, D])).then_inc(ln1_loaded, 16)
                    sp.dma_start(ln1b[:], ln1_b[0:1].to_broadcast([P, D])).then_inc(ln1_loaded, 16)
                    sp.dma_start(p_tok[:], p[0, 0].rearrange("(t q) d -> q t d", q=P)).then_inc(p_loaded, 16)
                if b == last["wo"]:
                    sp.wait_ge(block_read, last["wa"] + 1)
                    sp.dma_start(pleb[:], b_ple_gate[0:1].to_broadcast([P, D])).then_inc(pleb_loaded, 16)
                    sp.wait_ge(block_done, last["wa"] + 1)
                    load_gu(0, bass.ds(0, 1))
                if b == last["pp"]:
                    load_gu(1, bass.ds(1, 1))
                if b == last["pg"] - 1:
                    sp.wait_ge(block_read, last["wo"] + 1)
                    load_dn(3, bass.ds(3, 1))
                    sp.wait_ge(tr_done, 12)
                    load_dn(0, bass.ds(0, 1))
                if b == last["pg"]:
                    load_dn(1, bass.ds(1, 1))
                    sp.wait_ge(lo_ready, last_slice_of[len(loads) - 4] + 1)
                    load_gu(2, bass.ds(2, 1))
            sp.wait_ge(h_ready, TT)
            load_dn(2, bass.ds(2, 1))
            sp.wait_ge(block_read, last["pp"] + 1)
            sp.dma_start(ln2g[:], ln2_g[0:1].to_broadcast([P, D])).then_inc(ln2_loaded, 16)
            sp.dma_start(ln2b[:], ln2_b[0:1].to_broadcast([P, D])).then_inc(ln2_loaded, 16)
            sp.wait_ge(lo_ready, len(slices))
            load_gu(3, bass.ds(3, 1))

            def quad_loads(r, i):
                for par in range(2):
                    for s_ in (2 * par, 2 * par + 1):
                        sp.wait_ge(gu_done, 32 * r + 4 * i + s_ - 3)
                        load_gu(s_, bass.ds(4 * i + s_, 1))
                    sp.wait_ge(dn_done, 32 * r + 4 * i + 2 * par - 2)
                    for s_ in (2 * par, 2 * par + 1):
                        load_dn(s_, bass.ds(4 * i + s_, 1))

            with sp.Fori(1, N_EXP // 4) as i:
                quad_loads(0, i)
            sp.wait_ge(rt_done, 1)
            again = sp.value_load(more[0:1, 0:1])
            with sp.If(again > 0):
                with sp.Fori(1, PASSES) as r:
                    with sp.Fori(0, N_EXP // 4) as i:
                        quad_loads(r, i)
            for t in range(TT):
                sp.wait_ge(h_ready, TT + t + 1)
                sp.dma_start(out[0, t * P:(t + 1) * P, :], h_tok[:, t, :]).then_inc(stored, 16)
            sp.wait_ge(stored, 16 * TT)

        @block.tensor
        def _(pe):
            mm, tr = nc.tensor.matmul, nc.tensor.transpose
            at_slice = [0]

            def slices_pe(n):
                for _ in range(n):
                    j = at_slice[0]
                    at_slice[0] += 1
                    b, kt = slices[j]
                    name, act_pair, kts, _, wd = blocks[b]
                    a_hi, a_lo = pairs[act_pair]
                    if kt == 0:
                        if b >= 2:
                            pe.wait_ge(block_read, b - 1)
                        if act_pair == "ya":
                            pe.wait_ge(ya_made, NC)
                        elif act_pair == "p":
                            pe.wait_ge(p_made, 1)
                    if act_pair in lo_before and blocks[b - 1][1] != act_pair and kt % 2 == 0:
                        pe.wait_ge(lo_made, lo_before[act_pair] + kt // 2 + 1)
                    pe.wait_ge(lo_ready, j + 1)
                    hi, lo = w_hi[:, j % RING, :], w_lo[:, j % RING, :]
                    cols = block_bank(b)
                    parts = ((a_hi, hi), (a_lo, hi), (a_hi, lo))
                    if name in NARROW:
                        wd = 2 * wd
                        parts = ((a_hi, hi), (a_lo, hi))
                    outs = []
                    if name in ("k", "q", "v", "qa"):
                        outs = [(cols[:, c * T:(c + 1) * T], c * P, None) for c in range(4)]
                    elif name == "kva":
                        outs = [(cols[:, c * T:(c + 1) * T], c * P, None) for c in range(2)]
                        outs += [(cols[:, 512 + t * 256:768 + t * 256], 256, t) for t in range(TT)]
                    else:
                        outs = [(cols[:, t * 512:t * 512 + wd], 0, t) for t in range(TT)]
                    seen = set()
                    for o, c0, t in outs:
                        bank = c0 // 256 if t is None else ("b" if name == "kva" else t)
                        for q, (a, w_) in enumerate(parts):
                            begin = kt == 0 and q == 0 and bank not in seen
                            seen.add(bank)
                            end = kt == kts - 1 and q == len(parts) - 1
                            if t is None:
                                ins = mm(o, w_[:, c0:c0 + P], a[:, kt, :], start=begin, stop=end, skip_group_check=True)
                            else:
                                ins = mm(o, a[:, kt, t * P:(t + 1) * P], w_[:, c0:wd], start=begin, stop=end,
                                         skip_group_check=True)
                    if kt == kts - 1:
                        ins.then_inc(block_done, 1)
                        pe.wait_ge(block_done, b + 1)
                        pe.nop().then_inc(slice_used, 1)
                    else:
                        ins.then_inc(slice_used, 1)

            def turn_tokens(src, banks=range(4), tile_ready=None):
                def turn(q, k, t):
                    return tr(xbank[:, q * 512 + k * T + t * P:q * 512 + k * T + (t + 1) * P],
                              src[:, t, (2 * q + k) * P:(2 * q + k + 1) * P], ident[:])
                if tile_ready:
                    pe.wait_ge(tile_ready, 1)
                    for q in banks:
                        for k in range(2):
                            turn(q, k, 0)
                    pe.wait_ge(tile_ready, TT)
                for q in banks:
                    for k in range(2):
                        for t in range(1 if tile_ready else 0, TT):
                            ins = turn(q, k, t)
                    ins.then_inc(tr_done, 1)

            pe.wait_ge(ident_ready, 1)
            for hf in range(2):
                pe.wait_ge(x_loaded[hf], 16)
                turn_tokens(x_tok, range(2 * hf, 2 * hf + 2))
            slices_pe(4)
            pe.wait_ge(small_loaded, 16 * 5)
            tr(xbank[:, 0:TAPS * 24], conv_rows[0:TAPS * 24, :], ident[0:TAPS * 24, 0:TAPS * 24]).then_inc(cw_tr, 1)
            slices_pe(24)
            pe.wait_ge(ab3, 1)
            pe.wait_ge(cw_ready, 1)
            pe.wait_ge(consts, 1)
            for t in range(TT):
                mm(xbank[:, t * H:(t + 1) * H], tri[:], decay_g[:, t, :], start=True, stop=True)
                mm(xbank[:, 16 + t * H:16 + (t + 1) * H], chunk1[:], decay_g[:, t, :], start=True, stop=True)
                for b in range(2):
                    ins = mm(xbank[:, 32 + (2 * t + b) * H:40 + (2 * t + b) * H], half_rows[:, b, :], decay_g[:, t, :],
                             start=True, stop=True)
            ins.then_inc(cum_done, 1)

            def norm_sums(n):
                pe.wait_ge(squared, n + 1)
                if n == 0:
                    pe.wait_ge(cum_read, 1)
                if n >= 2:
                    pe.wait_ge(rs_ready, n - 1)
                for hh in range(2):
                    o0 = (n % 2) * 1024 + hh * 512
                    ins = mm(xbank[:, o0:o0 + 512], ones[:], sq[:, 2 * hh:2 * hh + 2, :], start=True, stop=True)
                ins.then_inc(sq_summed, 1)

            slices_pe(4)
            norm_sums(0)
            slices_pe(8)
            norm_sums(1)
            slices_pe(8)
            norm_sums(2)
            slices_pe(8)
            norm_sums(3)
            slices_pe(4)
            pe.wait_ge(beta_ready, 1)
            pe.wait_ge(rs_ready, 4)
            for h in range(H):
                for t in range(TT):
                    ins = mm(xbank[:, h * T + t * P:h * T + (t + 1) * P], bc(beta[:, t, h:h + 1], [P, P]), ident[:],
                             start=True, stop=True)
            ins.then_inc(brow, 1)
            slices_pe(4)
            pe.wait_ge(kb_ready, 1)
            for h in range(H):
                for t in range(TT):
                    ins = mm(xbank[:, h * T + t * P:h * T + (t + 1) * P], bc(decay_g[:, t, h:h + 1], [P, P]), tri[:],
                             start=True, stop=True)
            ins.then_inc(grow, 1)
            slices_pe(4)

            def gram_of(left, right, bank0):
                for h in range(H):
                    for t in range(TT):
                        for b in range(2):
                            tk = t * P + b * C
                            o0 = bank0 * 512 + (h * TT + t) * C
                            ins = mm(xbank[b * C:(b + 1) * C, o0:o0 + C], left[:, h, tk:tk + C], right[:, h, tk:tk + C],
                                     start=True, stop=True)
                ins.then_inc(gram, 1)

            pe.wait_ge(dec_raw, 1)
            gram_of(kT, kbT, 0)
            gram_of(kbT, kT, 2)
            slices_pe(2)
            pe.wait_ge(gram_read, 1)
            gram_of(kT, qT, 0)
            slices_pe(2)
            pe.wait_ge(conv_out, 6)
            pe.wait_ge(gram_read, 3)
            for src, done in ((vT, vtr), (kT, ktr)):
                for t in range(TT):
                    for h in range(H):
                        ins = tr(xbank[:, t * D + h * P:t * D + (h + 1) * P], src[:, h, t * P:(t + 1) * P], ident[:])
                    ins.then_inc(done, 1)
                slices_pe(2)
                if src is vT:
                    pe.wait_ge(vb_ready, TT)
            pe.wait_ge(kdec_ready, TT)

            def unit_products(bank0, left, right):
                for u in range(U):
                    for b in range(2):
                        rows = slice(b * C, (b + 1) * C)
                        o0 = bank0 * 512 + u * C
                        ins = mm(xbank[rows, o0:o0 + C], left[rows, u, :], right[rows, u, :], start=True, stop=True)
                return ins

            for lev in range(1, 6):
                pe.wait_ge(lev_masked, lev)
                pe.wait_ge(inv_ready, 2 * lev)
                unit_products(0, LT_lev[:, lev % 2], inv).then_inc(lev_prod, 1)
                slices_pe(2)
                pe.wait_ge(lev_copied, lev)
                if lev < 5:
                    unit_products(2, invT, prod).then_inc(lev_join, 1)
                slices_pe(1)
                unit_products(0, prod, invT).then_inc(lev_join, 1)
                slices_pe(1)

            def scan_a(n):
                t, b = n // 2, n % 2
                rows = slice(b * C, (b + 1) * C)
                tok = slice(n * C, (n + 1) * C)
                if n == 0:
                    pe.wait_ge(inv_ready, 11)
                    pe.wait_ge(eg_used, 2)
                else:
                    pe.wait_ge(s_ready, n)
                    pe.wait_ge(o_read, n)
                    for h in range(H):
                        ins = mm(xbank[rows, h * P:(h + 1) * P], kbT[:, h, tok], S[:, h, :], start=True, stop=True)
                    ins.then_inc(ks_done, 1)
                    for h in range(H):
                        ins = mm(xbank[rows, 1024 + h * P:1024 + (h + 1) * P], qT[:, h, tok], S[:, h, :],
                                 start=h % 4 == 0, stop=False, skip_group_check=True)
                    ins.then_inc(ks_done, 1)

            def scan_b(n):
                t, b = n // 2, n % 2
                rows = slice(b * C, (b + 1) * C)
                if n > 0:
                    pe.wait_ge(r_ready, n)
                for h in range(H):
                    rhs = vb[rows, t, h * P:(h + 1) * P] if n == 0 else R[rows, h * P:(h + 1) * P]
                    ins = mm(xbank[rows, h * P:(h + 1) * P], invT[rows, h * TT + t, :], rhs, start=True, stop=True)
                ins.then_inc(vn_done, 1)

            def scan_c(n):
                t, b = n // 2, n % 2
                rows = slice(b * C, (b + 1) * C)
                pe.wait_ge(vn_ready, n + 1)
                if n < NC - 1:
                    for h in range(H):
                        ins = mm(xbank[:, h * P:(h + 1) * P], kdec[rows, t, h * P:(h + 1) * P],
                                 v_new[rows, h * P:(h + 1) * P], start=True, stop=True)
                    ins.then_inc(ds_done, 1)
                for h in range(H):
                    ins = mm(xbank[rows, 1024 + h * P:1024 + (h + 1) * P], attT[rows, h * TT + t, :],
                             v_new[rows, h * P:(h + 1) * P], start=(n == 0 and h % 4 == 0), stop=True,
                             skip_group_check=True)
                ins.then_inc(o_done, 1)

            for n in range(NC):
                scan_a(n)
                slices_pe(SCAN_SLICES[n][0])
                scan_b(n)
                slices_pe(SCAN_SLICES[n][1])
                scan_c(n)
                slices_pe(SCAN_SLICES[n][2])

            def att_scores(c):
                if c == 0:
                    pe.wait_ge(block_read, kv_b + 1)
                elif c == 1:
                    pe.wait_ge(lo_made, 8)
                else:
                    pe.wait_ge(ya_made, c)
                for hp in range(HP):
                    g = hp // 2
                    for hh in range(2):
                        rows = slice(hh * C, (hh + 1) * C)
                        q_ = qaT[rows, hp, c * C:(c + 1) * C]
                        o = xbank[rows, hp * P:(hp + 1) * P]
                        if c == 0:
                            ins = mm(o[:, 0:C], q_, kaT[rows, g, 0:C], start=True, stop=True)
                        elif c % 2:
                            ins = mm(o, q_, kaT[rows, g, (c - 1) * C:(c + 1) * C], start=True, stop=True)
                        else:
                            mm(o[:, 0:C], q_, kaT[rows, g, c * C:(c + 1) * C], start=True, stop=True)
                            ins = mm(o[:, C:P], q_, kaT[rows, g, (c - 1) * C:c * C], start=True, stop=True)
                ins.then_inc(sc_done, 1)

            def att_turn(c):
                kk = C if c == 0 else P
                if c == 0:
                    pe.wait_ge(o_read, NC)
                for hp in range(HP):
                    if hp % (HP // 2) == 0:
                        pe.wait_ge(pr_ready, 2 * c + 2 * hp // HP + 1)
                    ins = tr(xbank[0:kk, 1024 + hp * P:1024 + (hp + 1) * P], pr[:, hp, 0:kk], ident[:])
                ins.then_inc(pt_done, 1)

            def att_pv(c):
                kk = C if c == 0 else P
                vt = (0, 0, 2, 1)[c]
                pe.wait_ge(pt_read, c + 1)
                for g in range(KVH):
                    for hh in range(2):
                        rows = slice(hh * C, (hh + 1) * C)
                        ins = mm(xbank[rows, 2 * g * C:(2 * g + 2) * C], va[0:kk, vt, g * C:(g + 1) * C],
                                 prT[0:kk, 2 * g:2 * g + 2, hh * C:(hh + 1) * C], start=True, stop=True)
                ins.then_inc(pv_done, 1)

            for c in range(NC):
                att_scores(c)
                slices_pe(ATT_SLICES[c][0])
                att_turn(c)
                slices_pe(ATT_SLICES[c][1])
                att_pv(c)
                slices_pe(ATT_SLICES[c][2])
                if c == 0:
                    slices_pe(TURN_SLICES)
                    pe.wait_ge(ya_made, 1)
                    pe.wait_ge(o_final, TT)
                    turn_tokens(o_tok)
                    slices_pe(2)
            slices_pe(wa_mid - at_slice[0])
            pe.wait_ge(ya_made, NC)
            pe.wait_ge(p_loaded, 16)
            for k in range(2):
                for t in range(TT):
                    ins = tr(xbank[:, 1536 + k * T + t * P:1536 + k * T + (t + 1) * P], p_tok[:, t, k * P:(k + 1) * P],
                             ident[:])
            ins.then_inc(p_turned, 1)
            slices_pe(1)
            pe.wait_ge(merged_ready, 1)
            turn_tokens(merged, range(2))
            slices_pe(wo_mid - at_slice[0])
            pe.wait_ge(p_made, 1)
            pe.wait_ge(merged_ready, 2)
            turn_tokens(merged, range(2, 4))
            slices_pe(pp_mid - at_slice[0])
            turn_tokens(h_tok, tile_ready=h_ready)
            slices_pe(1)
            slices_pe(11)
            slices_pe(5)
            pe.wait_ge(rt_picked, 1)
            pe.wait_ge(lo_made, 16)
            mm(xbank[:, 0:N_EXP], before[:], picked[:, 0, :], start=True, stop=True)
            mm(xbank[:, N_EXP:2 * N_EXP], ones[:], picked[:, 0, :], start=True, stop=False, skip_group_check=True)
            mm(xbank[:, N_EXP:2 * N_EXP], before[:], picked[:, 1, :], start=False, stop=True, skip_group_check=True)
            mm(xbank[:, 2 * N_EXP:3 * N_EXP], ones[:], picked[:, 0, :], start=True, stop=False, skip_group_check=True)
            mm(xbank[:, 2 * N_EXP:3 * N_EXP], ones[:], picked[:, 1, :], start=False, stop=True,
               skip_group_check=True).then_inc(rt_cum, 1)
            slices_pe(len(slices) - at_slice[0])
            pe.wait_ge(rt_done, 1)
            pe.wait_ge(block_read, len(blocks) - 1)
            pe.wait_ge(hk_ready, TT)

            def gather(step, part, a):
                wait(pe, gath_ready, step - 1)
                for k in range(4 * part + 2 * a, 4 * part + 2 * a + 2):
                    for t in range(TT):
                        for hk in (hk_hi, hk_lo):
                            ins = mm(dbank[:, a * 512 + (k % 2) * 256:a * 512 + (k % 2 + 1) * 256],
                                     hk[:, t, k * P:(k + 1) * P], sel_quad[:, t, :],
                                     start=(k % 2 == 0 and t == 0 and hk is hk_hi), stop=(t == 1 and hk is hk_lo),
                                     skip_group_check=True)
                ins.then_inc(gather_done, 1)

            def turn_sel(g, e):
                pe.wait_ge(sel_ready, g + 1)
                for t in range(TT):
                    tr(psD[:, 2, t * P:(t + 1) * P], sel[:, t, :].bitcast(F32), ident[:])
                for t in range(TT):
                    ins = mm(psD[:, 2, 256:258], sel[:, t, :].bitcast(F32), comb[:, t, e], start=t == 0, stop=t == 1,
                             skip_group_check=True)
                ins.then_inc(selt_done, 1)

            def scatter(m, par, hf):
                pe.wait_ge(ylo_ready, 2 * m + hf + 1)
                for t in range(TT):
                    if hf:
                        pe.wait_ge(acc_added, 4 * m + 2 + t)
                    for part in (y_hi, y_lo):
                        ins = mm(psX[:, t, :], selT[:, par, t, :], part[:, hf * W:(hf + 1) * W],
                                 start=part is y_hi, stop=part is y_lo)
                    ins.then_inc(sc_out, 1)

            def expert_pair(r, i, q, first=False):
                par, half = q % 2, q // 2
                n = 16 * r + 4 * i + q
                g = 17 * r + 4 * i + q
                step = 36 * r + 8 * i + 2 * q + 4
                if par == 0:
                    pe.wait_ge(gath_ready, step)
                pe.wait_ge(selt_ready, g + 1)
                for a in range(2):
                    pe.wait_ge(gu_load[2 * par + a], 256 * r + 64 * i + 32 * half + 32)
                    for k in range(KT):
                        rows = slice((k % 2) * C, (k % 2 + 1) * C)
                        ins = mm(psD[rows, 2 + a, :], gath[:, half, k, (2 * par + a) * C:(2 * par + a + 1) * C],
                                 w_gu[2 * par + a][:, k].rearrange("p j n -> p (j n)"), start=k < 2, stop=k >= KT - 2,
                                 skip_group_check=True)
                    ins.then_inc(gu_done, 1)
                    if not first:
                        scatter(n - 1, 1 - par, a)
                if par == 0:
                    pe.wait_ge(quad_ready, 9 * r + 2 * i + half + 2)
                gather(step, par, 0)
                for a in range(2):
                    pe.wait_ge(gus_ready, 2 * n + a + 1)
                    if a == 0:
                        pe.wait_ge(acc_added, 4 * n + 1)
                    for f in range(4):
                        ins = mm(psX[:, a, f * C:(f + 1) * C], gus[:, a, f * P:(f + 1) * P], stack_eye[:],
                                 start=True, stop=True)
                    ins.then_inc(t_done, 1)
                gather(step + 1, par, 1)
                turn_sel(g + 1, bass.ds(8 * i + 2 * q + 2, 2))
                pe.wait_ge(he_ready, 2 * n + 2)
                for hf in range(2):
                    for k in range(2):
                        for a in range(2):
                            if hf == 0 and k == 0:
                                pe.wait_ge(dn_load[2 * par + a], 128 * r + 32 * i + 16 * half + 16)
                            ins = mm(psX[a * C:(a + 1) * C, 2 + hf, :], he[:, a, k, :],
                                     w_dn[2 * par + a][:, k, hf * W:(hf + 1) * W], start=k == 0, stop=k == 1,
                                     skip_group_check=True)
                    ins.then_inc(dn_done, 1)

            def expert_pass(r):
                pe.wait_ge(quad_ready, 9 * r + 1)
                for part in range(2):
                    for a in range(2):
                        gather(36 * r + 2 * part + a, part, a)
                if isinstance(r, int):
                    pe.wait_ge(block_read, len(blocks))
                else:
                    pe.wait_ge(selt_ready, 17 * r)
                turn_sel(17 * r, slice(0, 2))
                for q in range(4):
                    expert_pair(r, 0, q, first=q == 0)
                with pe.Fori(1, N_EXP // 8) as i:
                    for q in range(4):
                        expert_pair(r, i, q)
                for hf in range(2):
                    scatter(16 * r + 15, 1, hf)

            expert_pass(0)
            again = pe.value_load(more[0:1, 0:1])
            with pe.If(again > 0):
                with pe.Fori(1, PASSES) as r:
                    expert_pass(r)

        @block.scalar
        def _(act):
            link, settle = chain(act, act_s)
            fn = nc.scalar.activation
            at_slice = [0]
            for dst, src in ((alog, a_log), (dtb, dt_bias)):
                act.dma_start(dst[:], src[0:1].to_broadcast([P, H])).then_inc(small_loaded, 16)
            act.dma_start(norm_g[:], gdn_norm_g[0:1].to_broadcast([P, P])).then_inc(small_loaded, 16)
            act.dma_start(conv_rows[0:TAPS * 24, :], conv_w[0].rearrange("k (c q) -> (k c) q", q=P)
                          ).then_inc(small_loaded, 16)
            act.dma_start(sink_all[:], attn_sink[0:1].to_broadcast([P, 2 * HP])).then_inc(small_loaded, 16)
            act.dma_start(rt_b[:, 0:N_GRP], b_route_group[0:1].to_broadcast([P, N_GRP])).then_inc(bias_loaded, 16)
            act.dma_start(rt_b[:, N_GRP:], b_route_expert[0:1].to_broadcast([P, N_EXP])).then_inc(bias_loaded, 16)

            def evacuate(b):
                name, _, _, off, wd = blocks[b]
                n = b - names.index(name)
                cols = block_bank(b)
                chan = cols.rearrange("p (c t) -> p c t", c=4)
                tok = cols.rearrange("p (t n) -> p t n", t=TT)
                if reader[name] == "scalar":
                    readers_in_order(act, b)
                if reader[name] == "scalar" or name == "z":
                    act.wait_ge(block_done, b + 1)
                if name in ("k", "q", "v"):
                    if b >= 3:
                        act.wait_ge(conv_ready, b - 2)
                    fn(conv_in[:, b % 2, :, TAPS - 1:], chan, ACT.Copy).then_inc(block_read, 1)
                elif name == "qa":
                    fn(qaT[:, 4 * n:4 * n + 4, :], chan, ACT.Copy, scale=0.125).then_inc(block_read, 1)
                elif name == "kva":
                    for hs in range(2):
                        for hh in range(2):
                            fn(kaT[hh * C:(hh + 1) * C].rearrange("p (c s) t -> p s c t", s=2)[:, hs],
                               chan[hs * C:(hs + 1) * C, 0:2, :], ACT.Copy)
                    fn(va[:, 0:2, :], chan[:, 2:4, :], ACT.Copy)
                    fn(va[0:C, 2, :], chan[0:C, 3, :], ACT.Copy)
                    link(fn(va[C:P, 2, :], chan[C:P, 2, :], ACT.Copy))
                    settle()
                    act.nop().then_inc(block_read, 1)
                elif name == "z":
                    if n == 0:
                        act.wait_ge(conv_out, 6)
                    fn(zg[:, :, n * W:(n + 1) * W], tok, ACT.Tanh, scale=0.5).then_inc(z_th, 1)
                elif name == "pp":
                    fn(acc[:, :, n * W:(n + 1) * W], tok, ACT.Copy, scale=0.5).then_inc(block_read, 1)
                elif name in ("ga", "gb"):
                    if name == "ga" and n == 0:
                        act.wait_ge(eg_used, 2)
                    if name == "gb" and n == 0:
                        act.wait_ge(o_summed, 1)
                    fn((th_a if name == "ga" else th_b)[:, :, n * W:(n + 1) * W], tok, ACT.Tanh,
                       scale=0.5).then_inc(block_read, 1)

            def finish(b):
                name = names[b]
                if name in ("k", "q", "v"):
                    act.wait_ge(conv_ready, b)
                    fn(conv_t[:], conv_y[:], ACT.Tanh, scale=0.5).then_inc(conv_th, 1)
                elif name == "pg":
                    n = b - names.index(name)
                    act.wait_ge(pg_in, n + 1)
                    fn(th_p[:, :, n * W:(n + 1) * W], th_p[:, :, n * W:(n + 1) * W], ACT.Tanh,
                       scale=0.5).then_inc(pg_th, 1)

            def slices_act(n):
                for _ in range(n):
                    j = at_slice[0]
                    at_slice[0] += 1
                    if j < len(slices):
                        m, q = place[j]
                        if q == 0:
                            act.wait_ge(load_sem[raw_place[m]], load_count(m))
                        if j >= RING:
                            act.wait_ge(slice_used, j - RING + 1)
                        fn(split_slice(j)[0], raw_slice(j), ACT.Copy).then_inc(hi_ready, 1)
                    if j - LEAD in end_slice:
                        evacuate(end_slice[j - LEAD])
                    if j - LEAD - 4 in end_slice:
                        finish(end_slice[j - LEAD - 4])

            def pair_hi(name, n, banks=range(4)):
                hi = pairs[name][0]
                for q in banks:
                    act.wait_ge(tr_done, 4 * n + q + 1)
                    fn(hi[:, 2 * q:2 * q + 2, :], psX[:, q, :].rearrange("p (k t) -> p k t", k=2),
                       ACT.Copy).then_inc(hi_made, 1)

            slices_act(1)
            pair_hi("x", 0)
            slices_act(LEAD - 1)
            slices_act(4)
            act.wait_ge(cw_tr, 1)
            fn(conv_c[:], xbank[:, 0:TAPS * 24].rearrange("p (k c) -> p k c", k=TAPS), ACT.Copy).then_inc(cw_ready, 1)
            act.wait_ge(small_loaded, 16 * 5)
            by_half = sink_all[:].rearrange("p (q two) -> p two q", two=2)
            for hh in range(2):
                ins = fn(sink[hh * C:(hh + 1) * C, :], by_half[hh * C:(hh + 1) * C, hh, :], ACT.Copy)
            ins.then_inc(sink_ready, 1)
            act.wait_ge(biases_ready, 1)
            slices_act(16)
            act.wait_ge(ab1, 1)
            link(fn(softb[:], softb[:], ACT.Exp, scale=-1.0))
            settle()
            fn(softb[:], softb[:], ACT.Ln, bias=one[:, 0:1])
            fn(neg_a[:], alog[:], ACT.Exp)
            fn(beta[:], ab[:, :, 0:H], ACT.Exp, scale=-1.0).then_inc(ab2, 1)
            slices_act(8)
            act.wait_ge(cum_read, 1)
            fn(to_end[:], to_end[:], ACT.Exp)
            fn(g_chunk[:], g_chunk[:], ACT.Exp).then_inc(cum_exp, 1)

            def norm_rs(n):
                act.wait_ge(sq_summed, n + 1)
                if n >= 2:
                    act.wait_ge(normed, n - 1)
                src = xbank[:, (n % 2) * 1024:(n % 2) * 1024 + 1024].rearrange("p (c t) -> p c t", c=4)
                scale = 1.0 if n < 2 else float(P)
                link(fn(rs[:, n % 2], src, ACT.Ln, bias=eps_l2[:, n // 2:n // 2 + 1], scale=scale))
                settle()
                fn(rs[:, n % 2], rs[:, n % 2], ACT.Exp, scale=-0.5).then_inc(rs_ready, 1)

            slices_act(4)
            norm_rs(0)
            slices_act(8)
            norm_rs(1)
            slices_act(8)
            norm_rs(2)
            slices_act(8)
            norm_rs(3)
            slices_act(4)
            slices_act(4)
            act.wait_ge(grow, 1)
            act.wait_ge(z_free, 1)
            fn(eg[:], xbank[:].rearrange("p (h t) -> p h t", h=H), ACT.Exp).then_inc(eg_ready, 1)
            slices_act(4)
            act.wait_ge(dec_masked, 2)
            fn(dec_sub[:], dec_sub[:], ACT.Exp)
            fn(dec_up[:], dec_up[:], ACT.Exp).then_inc(dec_ready, 1)
            slices_act(2)
            slices_act(2)
            slices_act(2)
            slices_act(2)
            for lev in range(1, 6):
                act.wait_ge(lev_prod, lev)
                fn(prod[:], xbank[:, 0:1024].rearrange("p (u c) -> p u c", u=U), ACT.Copy).then_inc(lev_copied, 1)
                slices_act(4)
            for n in range(NC):
                t, b = n // 2, n % 2
                rows = slice(b * C, (b + 1) * C)
                slices_act(SCAN_SLICES[n][0])
                act.wait_ge(vn_done, n + 1)
                fn(v_new[rows, :], xbank[rows, 0:1024], ACT.Copy).then_inc(vn_ready, 1)
                slices_act(SCAN_SLICES[n][1])
                act.wait_ge(o_done, n + 1)
                fn(o_tok[rows, t, :], xbank[rows, 1024:2048], ACT.Copy).then_inc(o_read, 1)
                if n == NC - 1:
                    act.wait_ge(o_read, NC)
                    fn(o_sq[:, 1, :], o_tok[:, 1, :], ACT.Square).then_inc(o_squared_act, 1)
                slices_act(SCAN_SLICES[n][2])
            for c in range(NC):
                kk = C if c == 0 else P
                for i_, hv in enumerate(HALVES):
                    act.wait_ge(sc_shift, 2 * c + i_ + 1)
                    if i_ == 0:
                        fn(sexp[:, 0, :], sexp[:, 0, :], ACT.Exp)
                    fn(pr[:, hv, 0:kk], pr[:, hv, 0:kk], ACT.Exp).then_inc(sc_exp, 1)
                slices_act(ATT_SLICES[c][0])
                act.wait_ge(pt_done, c + 1)
                fn(prT[0:kk], xbank[0:kk, 1024:2048].rearrange("p (c t) -> p c t", c=HP), ACT.Copy).then_inc(pt_read, 1)
                if c == 0:
                    act.wait_ge(o_summed, 1)
                    link(fn(o_rs[:], o_sum[:], ACT.Ln, scale=1.0 / P, bias=eps_norm[:, 0:1]))
                    settle()
                    fn(o_rs[:], o_rs[:], ACT.Exp, scale=-0.5).then_inc(o_rs_ready, 1)
                slices_act(ATT_SLICES[c][1])
                act.wait_ge(pv_done, c + 1)
                fn(pairs["ya"][0][:, :, c * C:(c + 1) * C], xbank[:, 0:512].rearrange("p (c t) -> p c t", c=HP),
                   ACT.Copy).then_inc(ya_hi, 1)
                slices_act(ATT_SLICES[c][2])
                if c == 0:
                    slices_act(TURN_SLICES)
                    pair_hi("yb", 1)
                    slices_act(2)
            slices_act(wa_mid + LEAD - at_slice[0])
            act.wait_ge(p_turned, 1)
            fn(pairs["p"][0][:], psX[:, 3, :].rearrange("p (k t) -> p k t", k=2), ACT.Copy).then_inc(p_hi, 1)
            slices_act(1)
            pair_hi("m", 2, range(2))
            slices_act(wo_mid + LEAD - at_slice[0])
            pair_hi("m", 2, range(2, 4))
            slices_act(first_slice[last["wo"] + 1] + LEAD - at_slice[0])

            def norm_rstd(n):
                for t in range(TT):
                    act.wait_ge(ln_var, TT * n + t + 1)
                    link(fn(rstd[:, t:t + 1], mv[:, t, 1:2], ACT.Ln, bias=eps_ln[:, 0:1]))
                    settle()
                    fn(rstd[:, t:t + 1], rstd[:, t:t + 1], ACT.Exp, scale=-0.5).then_inc(ln_rstd, 1)

            norm_rstd(0)
            slices_act(pp_mid + LEAD - at_slice[0])
            pair_hi("h", 3)
            for t in range(TT):
                fn(hk_hi[:, t, :], h_tok[:, t, :], ACT.Copy).then_inc(hk_hi_ready, 1)
            slices_act(1)
            slices_act(11)
            act.wait_ge(rt_in, 1)
            fn(g8[:, :, 0:N_GRP], g8[:, :, 0:N_GRP], ACT.Exp)
            fn(r_small[:, 0, :], r_small[:, 0, :], ACT.Exp).then_inc(rt_exp, 1)
            slices_act(4)
            slices_act(len(slices) + LEAD - at_slice[0])
            finish(len(blocks) - 1)

            def take_gather(step, buf, part, a):
                act.wait_ge(gather_done, step + 1)
                k0 = 4 * part + 2 * a
                fn(gath[:, buf, k0:k0 + 2, :], psD[:, a, :].rearrange("p (k s) -> p k s", k=2),
                   ACT.Copy).then_inc(gath_ready, 1)

            def take_sel(g, par):
                act.wait_ge(selt_done, g + 1)
                fn(selT[:, par], psD[:, 2, 0:256].rearrange("p (t s) -> p t s", t=TT), ACT.Copy)
                for a in range(2):
                    ins = fn(w_slot[a * C:(a + 1) * C, par:par + 1], psD[a * C:(a + 1) * C, 2, 256 + a:257 + a], ACT.Copy)
                ins.then_inc(selt_ready, 1)

            def expert_pass(r):
                for part in range(2):
                    for a in range(2):
                        take_gather(36 * r + 2 * part + a, 0, part, a)
                take_sel(17 * r, 0)
                with act.Fori(0, N_EXP // 8) as i:
                    for q in range(4):
                        par, half = q % 2, q // 2
                        n = 16 * r + 4 * i + q
                        g = 17 * r + 4 * i + q
                        step = 36 * r + 8 * i + 2 * q + 4
                        take_gather(step, 1 - half, par, 0)
                        for a in range(2):
                            act.wait_ge(t_done, 2 * n + a + 1)
                            fn(sg[:, a], psX[:, a, 0:2 * C].rearrange("p (k s) -> p k s", k=2), ACT.Silu
                               ).then_inc(silu_done, 1)
                        take_gather(step + 1, 1 - half, par, 1)
                        take_sel(g + 1, 1 - par)
                        for hf in range(2):
                            act.wait_ge(dn_done, 2 * n + hf + 1)
                            fn(y_hi[:, hf * W:(hf + 1) * W], psX[:, 2 + hf, :], ACT.Copy,
                               scale=w_slot[:, par:par + 1]).then_inc(yhi_ready, 1)

            expert_pass(0)
            act.wait_ge(rt_done, 1)
            again = act.value_load(more[0:1, 0:1])
            with act.If(again > 0):
                with act.Fori(1, PASSES) as r:
                    expert_pass(r)
            norm_rstd(1)

        @block.vector
        def _(dve):
            v = nc.vector
            link, settle = chain(dve, vec)
            at_slice = [0]

            def evacuate(b):
                name, _, _, off, wd = blocks[b]
                n = b - names.index(name)
                cols = block_bank(b)
                tok = cols.rearrange("p (t n) -> p t n", t=TT)
                c0 = n * W
                if reader[name] == "vector":
                    readers_in_order(dve, b)
                if name == "ab":
                    dve.wait_ge(block_done, b + 1)
                    link(v.tensor_copy(ab[:], tok[:, :, 0:wd]))
                    settle()
                    v.tensor_tensor(ab[:], ab[:], tok[:, :, wd:2 * wd], ALU.add).then_inc(block_read, 1)
                elif name in ("k", "q", "v"):
                    if b == 1:
                        dve.wait_ge(cw_ready, 1)
                    dve.wait_ge(block_read, b + 1)
                    if b > 1:
                        dve.wait_ge(conv_out, b - 1)
                    xin = conv_in[:, b % 2]
                    ct0 = {"q": 0, "k": 8, "v": 16}[name] + 4 * n
                    for tap in range(TAPS):
                        for c in range(4):
                            wt = conv_c[:, tap, ct0 + c:ct0 + c + 1]
                            src = xin[:, c, tap:tap + T]
                            if tap == 0:
                                ins = link(v.tensor_scalar(conv_y[:, c, :], src, wt, None, ALU.mult))
                            else:
                                ins = v.scalar_tensor_tensor(conv_y[:, c, :], src, wt, conv_y[:, c, :], ALU.mult, ALU.add)
                                if tap < TAPS - 1:
                                    link(ins)
                        if tap < TAPS - 1:
                            settle()
                    ins.then_inc(conv_ready, 1)
                elif name == "z":
                    dve.wait_ge(z_th, n + 1)
                    v.scalar_tensor_tensor(zg[:, :, c0:c0 + W], zg[:, :, c0:c0 + W], 1.0, tok, ALU.add, ALU.mult
                                           ).then_inc(block_read, 1)
                elif name == "wb":
                    dve.wait_ge(block_done, b + 1)
                    dve.wait_ge(block_read, last["gb"] + 1)
                    v.scalar_tensor_tensor(merged[:, :, c0:c0 + W], th_b[:, :, c0:c0 + W], 1.0, tok, ALU.add, ALU.mult
                                           ).then_inc(block_read, 1)
                elif name == "wa":
                    dve.wait_ge(block_done, b + 1)
                    for t in range(TT):
                        link(v.scalar_tensor_tensor(gated_a[:, t, :], th_a[:, t, c0:c0 + W], 1.0, tok[:, t, :], ALU.add,
                                                    ALU.mult))
                    settle()
                    v.engine_nop().then_inc(block_read, 1)
                    v.tensor_tensor(merged[:, :, c0:c0 + W], merged[:, :, c0:c0 + W], gated_a[:], ALU.add
                                    ).then_inc(merged_ready, 1)
                    if n == 0:
                        dve.wait_ge(merged_ready, 1)
                elif name == "wo":
                    dve.wait_ge(block_done, b + 1)
                    dve.wait_ge(ax_ready, 1)
                    for t in range(TT):
                        link(v.scalar_tensor_tensor(h_tok[:, t, c0:c0 + W], tok[:, t, :], 0.5, x_again[:, t, c0:c0 + W],
                                                    ALU.mult, ALU.add))
                        settle()
                        link(v.bn_stats(stats[:, t, n, :], h_tok[:, t, c0:c0 + W]))
                    v.engine_nop().then_inc(block_read, 1)
                elif name == "rt":
                    dve.wait_ge(block_done, b + 1)
                    dve.wait_ge(bias_loaded, 32)
                    link(v.tensor_tensor(lg[:], tok[:, :, 0:wd], rt_b[:].unsqueeze(1).to_broadcast([P, TT, wd]), ALU.add))
                    settle()
                    v.tensor_tensor(lg[:], lg[:], tok[:, :, wd:2 * wd], ALU.add).then_inc(block_read, 1)
                elif name == "pg":
                    dve.wait_ge(block_done, b + 1)
                    dve.wait_ge(pleb_loaded, 16)
                    for t in range(TT):
                        ins = v.tensor_tensor(th_p[:, t, c0:c0 + W], tok[:, t, :], pleb[:, c0:c0 + W], ALU.add)
                    ins.then_inc(block_read, 1)
                    dve.wait_ge(block_read, b + 1)
                    v.engine_nop().then_inc(pg_in, 1)

            def finish(b):
                name = names[b]
                n = b - names.index(name)
                if name in ("k", "q", "v"):
                    dst = {"k": kT, "q": qT, "v": vT}[name]
                    dve.wait_ge(conv_th, b)
                    v.scalar_tensor_tensor(dst[:, 4 * n:4 * n + 4, :], conv_t[:], 1.0, conv_y[:], ALU.add, ALU.mult
                                           ).then_inc(conv_out, 1)
                elif name == "pg":
                    dve.wait_ge(pg_th, n + 1)
                    cs = slice(n * W, (n + 1) * W)
                    link(v.scalar_tensor_tensor(acc[:, :, cs], th_p[:, :, cs], 1.0, acc[:, :, cs], ALU.add, ALU.mult))
                    settle()
                    v.scalar_tensor_tensor(acc[:, :, cs], h_tok[:, :, cs], ALPHA, acc[:, :, cs], ALU.mult, ALU.add
                                           ).then_inc(ple_added, 1)
                    if n:
                        dve.wait_ge(ple_added, 2)
                        v.engine_nop().then_inc(acc_added, 1)

            def slices_dve(n):
                for _ in range(n):
                    j = at_slice[0]
                    at_slice[0] += 1
                    if j < len(slices):
                        hi, lo = split_slice(j)
                        dve.wait_ge(hi_ready, j + 1)
                        v.tensor_tensor(lo, raw_slice(j), hi.bitcast(F32), ALU.subtract).then_inc(lo_ready, 1)
                    if j - LEAD in end_slice:
                        evacuate(end_slice[j - LEAD])
                    if j - LEAD - 4 in end_slice:
                        finish(end_slice[j - LEAD - 4])

            def pair_lo(name, n, banks=range(4)):
                hi, lo = pairs[name]
                for q in banks:
                    dve.wait_ge(hi_made, 4 * n + q + 1)
                    v.tensor_tensor(lo[:, 2 * q:2 * q + 2, :], psX[:, q, :].rearrange("p (k t) -> p k t", k=2),
                                    hi[:, 2 * q:2 * q + 2, :].bitcast(F32), ALU.subtract).then_inc(lo_made, 1)

            slices_dve(1)
            pair_lo("x", 0)
            slices_dve(LEAD - 1)
            slices_dve(16)
            dve.wait_ge(block_read, 1)
            dve.wait_ge(small_loaded, 16 * 5)
            link(v.tensor_tensor(soft[:], ab[:, :, H:2 * H], dtb_rows(), ALU.add))
            settle()
            v.scalar_tensor_tensor(softb[:], soft[:], -1.0, soft[:], ALU.mult, ALU.max).then_inc(ab1, 1)
            slices_dve(8)
            dve.wait_ge(ab2, 1)
            link(v.scalar_tensor_tensor(soft[:], soft[:], 0.0, softb[:], ALU.max, ALU.add))
            link(v.tensor_scalar(beta[:], beta[:], 1.0, None, ALU.add))
            settle()
            v.scalar_tensor_tensor(decay_g[:], soft[:], -1.0, neg_rows(), ALU.mult, ALU.mult).then_inc(ab3, 1)
            link(v.reciprocal(beta[:], beta[:]))
            settle()
            v.tensor_scalar(beta_half[:], beta[:], 0.5, None, ALU.mult).then_inc(beta_ready, 1)
            slices_dve(4)
            dve.wait_ge(cum_done, 1)
            link(v.tensor_copy(gc[:], xbank[:, 0:16].rearrange("p (t h) -> p t h", t=TT)))
            link(v.tensor_copy(g_chunk[:], xbank[:, 32:64].rearrange("p (n h) -> p n h", n=NC)))
            settle()
            v.tensor_tensor(to_end[:], xbank[:, 16:32].rearrange("p (t h) -> p t h", t=TT), gc[:], ALU.subtract
                            ).then_inc(cum_read, 1)

            slices_dve(4)
            slices_dve(8)
            slices_dve(8)
            slices_dve(8)
            slices_dve(4)
            dve.wait_ge(brow, 1)
            dve.wait_ge(normed, 4)
            v.tensor_tensor(kbT[:], kT[:], xbank[:].rearrange("p (h t) -> p h t", h=H), ALU.mult).then_inc(kb_ready, 1)
            slices_dve(4)
            dve.wait_ge(grow, 1)
            dve.wait_ge(eg_ready, 1)
            for b in range(2):
                rows = slice(b * C, (b + 1) * C)
                gview = gc[rows].rearrange("p t h -> p h t").unsqueeze(3).to_broadcast([C, H, TT, C])
                dview = dec_sub[rows].rearrange("p (h t) c -> p h t c", t=TT)
                rview = xbank[rows, :].rearrange("p (h t two c) -> p two h t c", t=TT, two=2, c=C)[:, b]
                ins = v.tensor_tensor(dview, gview, rview, ALU.subtract)
            ins.then_inc(dec_raw, 1)
            slices_dve(4)
            dve.wait_ge(gram, 1)
            dve.wait_ge(dec_ready, 1)
            uv = lambda b0: xbank[:, b0 * 512:b0 * 512 + 1024].rearrange("p (u c) -> p u c", u=U)
            eye_u = stack_eye[:].unsqueeze(1).to_broadcast([P, U, C])
            v.tensor_tensor(LT[:], uv(0), dec_up[:], ALU.mult).then_inc(gram_read, 1)
            dve.wait_ge(gram, 2)
            v.tensor_tensor(inv[:], uv(2), dec_sub[:], ALU.mult).then_inc(gram_read, 1)
            dve.wait_ge(gram_read, 2)
            v.tensor_tensor(inv[:], eye_u, inv[:], ALU.subtract).then_inc(inv_ready, 1)
            link(v.tensor_tensor(invT[:], LT[:], level_mask[:, 0:1, :].to_broadcast([P, U, C]), ALU.mult))
            settle()
            v.tensor_tensor(invT[:], eye_u, invT[:], ALU.subtract).then_inc(inv_ready, 1)
            slices_dve(2)
            dve.wait_ge(gram, 3)
            v.tensor_tensor(attT[:], uv(0), dec_up[:], ALU.mult).then_inc(gram_read, 1)
            slices_dve(2)
            for t in range(TT):
                dve.wait_ge(vtr, t + 1)
                v.tensor_tensor(vb[:, t, :].rearrange("p (h c) -> p h c", h=H),
                                xbank[:, t * D:(t + 1) * D].rearrange("p (h c) -> p h c", h=H),
                                beta_half[:, t, :].unsqueeze(2).to_broadcast([P, H, P]), ALU.mult).then_inc(vb_ready, 1)
            slices_dve(2)
            dve.wait_ge(cum_exp, 1)
            for t in range(TT):
                dve.wait_ge(ktr, t + 1)
                v.tensor_tensor(kdec[:, t, :].rearrange("p (h c) -> p h c", h=H),
                                xbank[:, t * D:(t + 1) * D].rearrange("p (h c) -> p h c", h=H),
                                to_end[:, t, :].unsqueeze(2).to_broadcast([P, H, P]), ALU.mult).then_inc(kdec_ready, 1)
            slices_dve(2)
            for lev in range(1, 6):
                slices_dve(2)
                if lev < 5:
                    dve.wait_ge(lev_join, 2 * lev - 1)
                    v.tensor_tensor(inv[:], inv[:], uv(2), ALU.subtract).then_inc(inv_ready, 1)
                dve.wait_ge(lev_join, min(2 * lev, 9))
                v.tensor_tensor(invT[:], invT[:], uv(0), ALU.subtract).then_inc(inv_ready, 1)
                slices_dve(2)
            for n in range(NC):
                t, b = n // 2, n % 2
                rows = slice(b * C, (b + 1) * C)
                if n > 0:
                    dve.wait_ge(ks_done, 2 * n - 1)
                    v.tensor_tensor(R[rows, :], vb[rows, t, :], xbank[rows, 0:1024], ALU.subtract).then_inc(r_ready, 1)
                slices_dve(SCAN_SLICES[n][0] + SCAN_SLICES[n][1])
                if n < NC - 1:
                    dve.wait_ge(ds_done, n + 1)
                    src = xbank[:, 0:1024].rearrange("p (h c) -> p h c", h=H)
                    if n == 0:
                        v.tensor_copy(S[:], src).then_inc(s_ready, 1)
                    else:
                        dve.wait_ge(s_scaled, n)
                        v.tensor_tensor(S[:], S[:], src, ALU.add).then_inc(s_ready, 1)
                slices_dve(SCAN_SLICES[n][2])
            for c in range(NC):
                kk = C if c == 0 else P
                scv = xbank[:, 0:1024].rearrange("p (c t) -> p c t", c=HP)[:, :, 0:kk]
                dve.wait_ge(sink_ready, 1)
                dve.wait_ge(sc_done, c + 1)
                if c:
                    dve.wait_ge(pt_done, c)
                    dve.wait_ge(sc_den, c)
                link(v.tensor_reduce(smax[:, 0, :], scv, AX_X, ALU.max))
                settle()
                link(v.tensor_tensor(smax[:, 1, :], smax[:, 0, :], sink[:], ALU.max))
                settle()
                link(v.tensor_tensor(sexp[:, 0, :], sink[:], smax[:, 1, :], ALU.subtract))
                settle()
                for hv in HALVES:
                    v.tensor_tensor(pr[:, hv, 0:kk], scv[:, hv], smax[:, 1, hv].unsqueeze(2).to_broadcast([P, HP // 2, kk]),
                                    ALU.subtract).then_inc(sc_shift, 1)
                slices_dve(1)
                for i_, hv in enumerate(HALVES):
                    dve.wait_ge(sc_exp, 2 * c + i_ + 1)
                    link(v.tensor_reduce(sden[:, 0, hv], pr[:, hv, 0:kk], AX_X, ALU.add))
                settle()
                link(v.tensor_tensor(sden[:, 1, :], sden[:, 0, :], sexp[:, 0, :], ALU.add))
                settle()
                v.reciprocal(sden[:, 0, :], sden[:, 1, :]).then_inc(sc_den, 1)
                dve.wait_ge(sc_den, c + 1)
                for hv in HALVES:
                    v.tensor_tensor(pr[:, hv, 0:kk], pr[:, hv, 0:kk],
                                    sden[:, 0, hv].unsqueeze(2).to_broadcast([P, HP // 2, kk]),
                                    ALU.mult).then_inc(pr_ready, 1)
                if c == 0:
                    dve.wait_ge(o_squared, 1)
                    dve.wait_ge(o_squared_act, 1)
                    v.tensor_reduce(o_sum[:], o_sq[:].rearrange("p t (h c) -> p t h c", h=H), AX_X, ALU.add
                                    ).then_inc(o_summed, 1)
                slices_dve(ATT_SLICES[c][0] + ATT_SLICES[c][1] - 1)
                dve.wait_ge(ya_hi, c + 1)
                hi, lo = pairs["ya"]
                v.tensor_tensor(lo[:, :, c * C:(c + 1) * C], xbank[:, 0:512].rearrange("p (c t) -> p c t", c=HP),
                                hi[:, :, c * C:(c + 1) * C].bitcast(F32), ALU.subtract).then_inc(ya_made, 1)
                if c == 0:
                    dve.wait_ge(o_rs_ready, 1)
                    for t in range(TT):
                        dve.wait_ge(o_gated, t + 1)
                        ov = o_tok[:, t, :].rearrange("p (h c) -> p h c", h=H)
                        v.tensor_tensor(ov, ov, o_rs[:, t, :].unsqueeze(2).to_broadcast([P, H, P]), ALU.mult
                                        ).then_inc(o_final, 1)
                slices_dve(ATT_SLICES[c][2])
                if c == 0:
                    slices_dve(TURN_SLICES)
                    pair_lo("yb", 1)
                    slices_dve(2)
            slices_dve(wa_mid + LEAD - at_slice[0])
            dve.wait_ge(p_hi, 1)
            v.tensor_tensor(pairs["p"][1][:], psX[:, 3, :].rearrange("p (k t) -> p k t", k=2),
                            pairs["p"][0][:].bitcast(F32), ALU.subtract).then_inc(p_made, 1)
            slices_dve(1)
            pair_lo("m", 2, range(2))
            slices_dve(wo_mid + LEAD - at_slice[0])
            pair_lo("m", 2, range(2, 4))
            slices_dve(first_slice[last["wo"] + 1] + LEAD - at_slice[0])

            def layer_norm(n, src, g_, b_, ready):
                settle()
                for t in range(TT):
                    v.bn_aggr(mv[:, t, :], stats[:, t].rearrange("p q s -> p (q s)")).then_inc(ln_var, 1)
                for t in range(TT):
                    dve.wait_ge(ln_var, TT * n + t + 1)
                    link(v.scalar_tensor_tensor(src[:, t, :], src[:, t, :], mv[:, t, 0:1], g_[:], ALU.subtract, ALU.mult))
                settle()
                for t in range(TT):
                    dve.wait_ge(ln_rstd, TT * n + t + 1)
                    v.scalar_tensor_tensor(h_tok[:, t, :], src[:, t, :], rstd[:, t:t + 1], b_[:], ALU.mult, ALU.add
                                           ).then_inc(ready, 1)

            dve.wait_ge(ln1_loaded, 32)
            layer_norm(0, h_tok, ln1g, ln1b, h_ready)
            slices_dve(pp_mid + LEAD - at_slice[0])
            pair_lo("h", 3)
            slices_dve(1)
            slices_dve(11)
            dve.wait_ge(block_read, last["rt"] + 1)
            for t in range(TT):
                link(v.tensor_copy(g8[:, t, 0:N_GRP], lg[:, t, 0:N_GRP]))
            settle()
            for t in range(TT):
                link(v.max(top8[:, t, 0, :], g8[:, t, :]))
            settle()
            for t in range(TT):
                link(v.max_index(idx8[:, t, 0, :], top8[:, t, 0, :], g8[:, t, :]))
            settle()
            link(v.tensor_copy(idxf[:, :, 0, :], idx8[:, :, 0, :]))
            settle()
            for t in range(TT):
                link(v.tensor_scalar(g_hot[:, t, :], iota_e[:, 0:N_GRP], idxf[:, t, 0, 0:1], None, ALU.is_equal))
                link(v.tensor_scalar(g8[:, t, 0:N_GRP], g8[:, t, 0:N_GRP], top8[:, t, 0, 0:1], None, ALU.subtract))
            settle()
            link(v.tensor_scalar(g_hot[:], g_hot[:], -1.0, BIG, ALU.add, ALU.mult))
            settle()
            for t in range(TT):
                link(v.tensor_tensor(e_mask[:, t], lg[:, t, N_GRP:].rearrange("p (g e) -> p g e", g=N_GRP),
                                     g_hot[:, t, :].unsqueeze(2).to_broadcast([P, N_GRP, EPG]), ALU.add))
            settle()
            for t in range(TT):
                link(v.max(top8[:, t, 1, :], e_mask[:, t].rearrange("p g e -> p (g e)")))
            settle()
            for t in range(TT):
                link(v.max_index(idx8[:, t, 1, :], top8[:, t, 1, :], e_mask[:, t].rearrange("p g e -> p (g e)")))
            settle()
            link(v.tensor_copy(idxf[:, :, 1, :], idx8[:, :, 1, :]))
            v.tensor_tensor(r_small[:, 0, :], top8[:, :, 1, 1], top8[:, :, 1, 0], ALU.subtract).then_inc(rt_in, 1)
            settle()
            for t in range(TT):
                for k in range(2):
                    link(v.tensor_scalar(hot[:, k, t, :], iota_e[:], idxf[:, t, 1, k:k + 1], None, ALU.is_equal))
            settle()
            v.tensor_tensor(picked[:], hot[:, 0], hot[:, 1], ALU.add).then_inc(rt_picked, 1)
            dve.wait_ge(rt_exp, 1)
            link(v.tensor_reduce(r_small[:, 1, :], g8[:, :, 0:N_GRP], AX_X, ALU.add))
            link(v.tensor_scalar(r_small[:, 2, :], r_small[:, 0, :], 1.0, None, ALU.add))
            settle()
            link(v.tensor_tensor(r_small[:, 3, :], r_small[:, 1, :], r_small[:, 2, :], ALU.mult))
            settle()
            link(v.reciprocal(r_small[:, 4, :], r_small[:, 3, :]))
            settle()
            link(v.tensor_tensor(r_small[:, 5, :], r_small[:, 4, :], r_small[:, 0, :], ALU.mult))
            settle()
            for t in range(TT):
                link(v.tensor_scalar(hot[:, 1, t, :], hot[:, 1, t, :], r_small[:, 5, t:t + 1], None, ALU.mult))
            settle()
            for t in range(TT):
                link(v.scalar_tensor_tensor(comb[:, t, 0:N_EXP], hot[:, 0, t, :], r_small[:, 4, t:t + 1],
                                            hot[:, 1, t, :], ALU.mult, ALU.add))
            slices_dve(5)
            dve.wait_ge(rt_cum, 1)
            pos = xbank[:, 0:2 * N_EXP].rearrange("p (t e) -> p t e", t=TT)
            dve.wait_ge(rt_picked, 1)
            link(v.scalar_tensor_tensor(posm[:, :, 0:N_EXP], pos, 1.0, picked[:], ALU.add, ALU.mult))
            link(v.tensor_reduce(n_max[:], xbank[:, 2 * N_EXP:3 * N_EXP], AX_X, ALU.max))
            settle()
            link(v.tensor_scalar(posm[:, :, 0:N_EXP], posm[:, :, 0:N_EXP], -1.0, None, ALU.add))
            settle()
            v.tensor_scalar(more[:], n_max[:], float(SLOTS), None, ALU.is_gt).then_inc(rt_done, 1)
            for t in range(TT):
                dve.wait_ge(hk_hi_ready, t + 1)
                v.tensor_tensor(hk_lo[:, t, :], h_tok[:, t, :], hk_hi[:, t, :].bitcast(F32), ALU.subtract
                                ).then_inc(hk_ready, 1)
            slices_dve(len(slices) + LEAD - 1 - at_slice[0])

            def select(g, e):
                v.tensor_tensor(sel[:].rearrange("p t (a s) -> p t a s", a=2),
                                iota_s[:].unsqueeze(1).unsqueeze(1).to_broadcast([P, TT, 2, SLOTS]),
                                posm[:, :, e].unsqueeze(3).to_broadcast([P, TT, 2, SLOTS]), ALU.is_equal
                                ).then_inc(sel_ready, 1)

            def select_quad(e):
                v.tensor_tensor(sel_quad[:].rearrange("p t (a s) -> p t a s", a=4),
                                iota_s[:].unsqueeze(1).unsqueeze(1).to_broadcast([P, TT, 4, SLOTS]),
                                posm[:, :, e].unsqueeze(3).to_broadcast([P, TT, 4, SLOTS]), ALU.is_equal
                                ).then_inc(quad_ready, 1)

            def expert_pass(r):
                if not isinstance(r, int):
                    dve.wait_ge(selt_done, 17 * r)
                    dve.wait_ge(gather_done, 36 * r)
                    dve.wait_ge(sel_ready, 17 * r)
                    dve.wait_ge(quad_ready, 9 * r)
                    v.tensor_scalar(posm[:], posm[:], -float(SLOTS), None, ALU.add).then_inc(pass_shift, 1)
                    dve.wait_ge(pass_shift, r)
                select_quad(slice(0, 4))
                select(17 * r, slice(0, 2))
                if isinstance(r, int):
                    slices_dve(1)
                    finish(len(blocks) - 1)

                def add_outputs(m, hf):
                    cs = slice(hf * W, (hf + 1) * W)
                    for t in range(TT):
                        dve.wait_ge(sc_out, 4 * m + 2 * hf + t + 1)
                        dve.wait_ge(acc_added, 4 * m + 1)
                        v.tensor_tensor(acc[:, t, cs], acc[:, t, cs], psX[:, t, :], ALU.add).then_inc(acc_added, 1)

                def expert_pair(i, q, first=False):
                    par, half = q % 2, q // 2
                    n = 16 * r + 4 * i + q
                    g = 17 * r + 4 * i + q
                    if par == 0:
                        dve.wait_ge(gather_done, 36 * r + 8 * i + 2 * q + 4)
                        select_quad(bass.ds(8 * i + 2 * q + 4, 4))
                    dve.wait_ge(selt_done, g + 1)
                    select(g + 1, bass.ds(8 * i + 2 * q + 2, 2))
                    for a in range(2):
                        dve.wait_ge(gu_done, 2 * n + a + 1)
                        v.tensor_copy(gus[:, a, :], psD[:, 2 + a, :]).then_inc(gus_ready, 1)
                        if not first:
                            add_outputs(n - 1, a)
                    for a in range(2):
                        dve.wait_ge(silu_done, 2 * n + a + 1)
                        v.tensor_tensor(he[:, a], psX[:, a, 2 * C:4 * C].rearrange("p (k s) -> p k s", k=2),
                                        sg[:, a], ALU.mult).then_inc(he_ready, 1)
                    for hf in range(2):
                        dve.wait_ge(yhi_ready, 2 * n + hf + 1)
                        cs = slice(hf * W, (hf + 1) * W)
                        v.scalar_tensor_tensor(y_lo[:, cs], psX[:, 2 + hf, :], w_slot[:, par:par + 1],
                                               y_hi[:, cs].bitcast(F32), ALU.mult, ALU.subtract
                                               ).then_inc(ylo_ready, 1)

                for q in range(4):
                    expert_pair(0, q, first=q == 0)
                with dve.Fori(1, N_EXP // 8) as i:
                    for q in range(4):
                        expert_pair(i, q)
                wait(dve, stats_made, 4 * r)
                for hf in range(2):
                    add_outputs(16 * r + 15, hf)
                    dve.wait_ge(acc_added, 64 * r + 63 + 2 * hf)
                    for t in range(TT):
                        v.bn_stats(stats[:, t, hf, :], acc[:, t, hf * W:(hf + 1) * W]).then_inc(stats_made, 1)

            dve.wait_ge(rt_done, 1)
            expert_pass(0)
            again = dve.value_load(more[0:1, 0:1])
            with dve.If(again > 0):
                with dve.Fori(1, PASSES) as r:
                    expert_pass(r)
                dve.wait_ge(acc_added, 64 * PASSES + 1)
                dve.wait_ge(stats_made, 4 * PASSES)
            dve.wait_ge(acc_added, 65)
            dve.wait_ge(stats_made, 4)
            dve.wait_ge(ln2_loaded, 32)
            layer_norm(1, acc, ln2g, ln2b, h_ready)

        @block.gpsimd
        def _(pool):
            g_ = nc.gpsimd
            count_up, settle = chain(pool, pool_s)

            def link(ins):
                count_up(ins)
                settle()

            def keep(t_, pattern, base, cm, fill=0.0, op=ALU.is_ge):
                link(g_.affine_select(out=t_, in_=t_, pattern=pattern, compare_op=op, fill=fill, base=base,
                                      channel_multiplier=cm))

            link(g_.memset(ident[:], 0.0))
            keep(ident[:], [[-1, P]], 0, 1, 1.0, ALU.not_equal)
            pool.nop().then_inc(ident_ready, 1)
            link(g_.memset(conv_in[:, :, :, 0:TAPS - 1], 0.0))
            link(g_.memset(eps_l2[:, 0:1], 4 * NORM_EPS))
            link(g_.memset(eps_l2[:, 1:2], 4 * NORM_EPS * P))
            link(g_.memset(eps_ln[:], LN_EPS))
            link(g_.memset(eps_norm[:], NORM_EPS))
            link(g_.memset(one[:], 1.0))
            pool.nop().then_inc(biases_ready, 1)
            for m in (ones, half_rows):
                link(g_.memset(m[:], 1.0))
            link(g_.memset(stack_eye[:], 0.0))
            link(g_.memset(tri[:], 1.0))
            link(g_.memset(before[:], 1.0))
            link(g_.memset(chunk1[:], 1.0))
            link(g_.memset(level_mask[:], 1.0))
            link(g_.memset(mask_upper[:], 0.0))
            link(g_.memset(mask_sub[:], -BIG))
            link(g_.memset(g8[:], -BIG))
            link(g_.memset(comb[:], 0.0))
            link(g_.memset(posm[:], -1.0))
            settle()

            keep(tri[:], [[1, P]], 0, -1)
            keep(before[:], [[1, P]], -1, -1)
            keep(half_rows[:, 0, :], [[0, P]], C - 1, -1)
            keep(half_rows[:, 1, :], [[0, P]], -C, 1)
            for b in range(2):
                keep(stack_eye[:], [[-1, C]], -b * C, 1, 1.0, ALU.not_equal)
                settle()
            settle()
            keep(tri[:, C:P], [[0, C]], -C, 1)
            keep(chunk1[:, C:P], [[0, C]], -C, 1)
            settle()
            keep(chunk1[:, 0:C], [[0, C]], C - 1, -1)
            for b in range(2):
                rows = slice(b * C, (b + 1) * C)
                keep(mask_upper[rows, :], [[1, C]], 0, -1, -BIG)
                keep(mask_sub[rows, :].rearrange("p (a two) -> p two a", two=2)[:, 0], [[-2, C // 2]], -1, 1, 0.0,
                     ALU.not_equal)
                for lev in range(6):
                    s_ = 1 << lev
                    m = level_mask[rows, lev, :].rearrange("p (a two s) -> p a two s", two=2, s=s_)
                    link(g_.memset(m[:, :, 0, :], 0.0))
                    for lo_, base, cm in ((True, 0, 1), (False, s_ - 1, -1)):
                        settle()
                        step = -2 * s_ if lo_ else 2 * s_
                        keep(m[:, :, 1, :], [[step, C // (2 * s_)], [0, s_]], base, cm)
            link(g_.iota(iota_e[:], [[1, N_EXP]], base=0, channel_multiplier=0, allow_small_or_imprecise_dtypes=True))
            link(g_.iota(iota_s[:], [[1, SLOTS]], base=0, channel_multiplier=0, allow_small_or_imprecise_dtypes=True))
            settle()
            pool.nop().then_inc(consts, 1)
            pool.wait_ge(small_loaded, 16 * 5)
            g_.tensor_scalar(norm_g[:], norm_g[:], 0.5, None, ALU.mult).then_inc(z_free, 1)
            for n in range(4):
                pool.wait_ge(conv_out, n + 1)
                if n:
                    pool.wait_ge(sq_summed, n)
                src = (kT if n < 2 else qT)[:, 4 * (n % 2):4 * (n % 2) + 4, :]
                g_.tensor_tensor(sq[:], src, src, ALU.mult).then_inc(squared, 1)
                pool.wait_ge(rs_ready, n + 1)
                g_.tensor_tensor(src, src, rs[:, n % 2], ALU.mult).then_inc(normed, 1)
            pool.wait_ge(dec_raw, 1)
            d4 = lambda m: m.unsqueeze(1).to_broadcast([P, U, C])
            g_.tensor_tensor(dec_up[:], d4(mask_upper[:]), dec_sub[:], ALU.subtract).then_inc(dec_masked, 1)
            g_.tensor_tensor(dec_sub[:], dec_sub[:], d4(mask_sub[:]), ALU.add).then_inc(dec_masked, 1)
            pool.wait_ge(gram, 3)
            pool.wait_ge(eg_ready, 1)
            for m in (kbT, qT):
                g_.tensor_tensor(m[:], m[:], eg[:], ALU.mult).then_inc(eg_used, 1)
            pool.wait_ge(gram_read, 3)
            for lev in range(1, 6):
                if lev > 2:
                    pool.wait_ge(lev_prod, lev - 2)
                g_.tensor_tensor(LT_lev[:, lev % 2], LT[:], d4(level_mask[:, lev, :]), ALU.mult).then_inc(lev_masked, 1)
            for n in range(1, NC - 1):
                pool.wait_ge(ks_done, 2 * n)
                g_.tensor_tensor(S[:], S[:], g_chunk[:, n, :].unsqueeze(2).to_broadcast([P, H, P]), ALU.mult
                                 ).then_inc(s_scaled, 1)
            for n in range(2):
                pool.wait_ge(block_read, names.index("z") + n + 1)
                zv = zg[:, :, n * W:(n + 1) * W].rearrange("p t (h c) -> p t h c", c=P)
                for t in range(TT):
                    ins = g_.tensor_tensor(zv[:, t], zv[:, t], norm_g[:].unsqueeze(1).to_broadcast([P, W // P, P]),
                                           ALU.mult)
                ins.then_inc(z_norm, 1)
            pool.wait_ge(ks_done, 2 * (NC - 1))
            g_.tensor_tensor(o_sq[:, 0, :], o_tok[:, 0, :], o_tok[:, 0, :], ALU.mult).then_inc(o_squared, 1)
            pool.wait_ge(z_norm, 2)
            pool.wait_ge(o_squared, 1)
            g_.tensor_tensor(o_tok[:, 0, :], o_tok[:, 0, :], zg[:, 0, :], ALU.mult).then_inc(o_gated, 1)
            pool.wait_ge(o_squared_act, 1)
            g_.tensor_tensor(o_tok[:, 1, :], o_tok[:, 1, :], zg[:, 1, :], ALU.mult).then_inc(o_gated, 1)
            pool.wait_ge(x2_loaded, 16)
            g_.tensor_scalar(x_again[:], x_again[:], ALPHA, None, ALU.mult).then_inc(ax_ready, 1)


_INS = ["x", "p", "w_in", "attn_sink", "conv_w", "a_log", "dt_bias", "gdn_norm_g", "w_branch_a", "w_branch_b",
        "w_out", "ln1_g", "ln1_b", "w_route_group", "b_route_group", "w_route_expert", "b_route_expert",
        "w_exp_gate", "w_exp_up", "w_exp_down", "w_ple_gate", "b_ple_gate", "w_ple_proj", "ln2_g", "ln2_b"]
_OUTS = [((1, 256, 1024), "float32")]


def kernel(**inputs):
    import numpy as _np
    import concourse.bacc as _bacc
    from concourse import mybir as _mybir
    from concourse.bass_utils import run_bass_kernel_spmd as _run

    nc = _bacc.Bacc("TRN2", target_bir_lowering=False, num_devices=1)
    arrays, args = {}, []
    for name in _INS:
        a = _np.ascontiguousarray(inputs[name])
        arrays[f"in_{name}_dram"] = a
        args.append(nc.dram_tensor(f"in_{name}_dram", a.shape, _mybir.dt.from_np(a.dtype), kind="ExternalInput").ap())
    for i, (shape, dtype) in enumerate(_OUTS):
        dt = _mybir.dt.from_np(_np.dtype(dtype))
        args.append(nc.dram_tensor(f"out_{i}_dram", shape, dt, kind="ExternalOutput").ap())
    build(nc, *args)
    r = _run(nc, [arrays], core_ids=[0])
    return r.results[0]["out_0_dram"]
```
